# Optimizing a Trainium2 kernel written in Bass

```python
import jax, jax.numpy as jnp
from jax import lax
import numpy as np

D_MODEL = 1024
BATCH = 1
SEQ = 512
DEPTH = 1

N_META = 16
GRID_W = 64
MLA_HEADS = 8
MLA_NOPE = 64
MLA_ROPE = 32
MLA_V = 64
MLA_QK = MLA_NOPE + MLA_ROPE
Q_LORA = 384
KV_LORA = 256
NA_HEADS = 8
NA_HEAD_DIM = 64
NA_MAX_ROWS = 8
NA_KW = 16
D_FF = 2816
Q_BLOCK = 128
ROPE_THETA = 10000.0
EPS = 1e-6
MLA_WIDTH = MLA_HEADS * MLA_V
NA_WIDTH = NA_HEADS * NA_HEAD_DIM
IN_SPLITS = (Q_LORA, KV_LORA, MLA_ROPE, NA_WIDTH, NA_WIDTH, NA_WIDTH, D_MODEL, D_MODEL)
IN_WIDTH = Q_LORA + KV_LORA + MLA_ROPE + 3 * NA_WIDTH + 2 * D_MODEL

kernel_name = 'hybrid_mla_natten_macaron_block'

def rmsnorm(x, g):
    xf = x.astype(jnp.float32)
    y = xf * lax.rsqrt(jnp.mean(xf * xf, axis=-1, keepdims=True) + EPS)
    return (y * g.astype(jnp.float32)).astype(x.dtype)

def swiglu(x, w_gate, w_up, w_down):
    return (jax.nn.silu(x @ w_gate) * (x @ w_up)) @ w_down

def rope_tables(t_len):
    half = MLA_ROPE // 2
    pos = jnp.arange(t_len, dtype=jnp.float32)
    inv = ROPE_THETA ** (-jnp.arange(half, dtype=jnp.float32) / half)
    ang = pos[:, None] * inv[None, :]
    return jnp.cos(ang), jnp.sin(ang)

def apply_rope(x, cos, sin):
    half = MLA_ROPE // 2
    c = cos[None, :, None, :].astype(x.dtype)
    s = sin[None, :, None, :].astype(x.dtype)
    x1, x2 = x[..., :half], x[..., half:]
    return jnp.concatenate([x1 * c - x2 * s, x1 * s + x2 * c], axis=-1)

def dense_attend(q, k, v, scale):
    s = jnp.einsum('bqhd,bkhd->bhqk', q, k).astype(jnp.float32) * scale
    p = jax.nn.softmax(s, axis=-1).astype(v.dtype)
    return jnp.einsum('bhqk,bkhd->bqhd', p, v)

def mla_mixer(c_q, c_kv, k_r, q_a_norm, w_uq, kv_a_norm, w_ukv, q_head_norm, k_head_norm):
    b, t_len, _ = c_q.shape
    q = (rmsnorm(c_q, q_a_norm) @ w_uq).reshape(b, t_len, MLA_HEADS, MLA_QK)
    kv = (rmsnorm(c_kv, kv_a_norm) @ w_ukv).reshape(b, t_len, MLA_HEADS, MLA_NOPE + MLA_V)
    k_nope, v = kv[..., :MLA_NOPE], kv[..., MLA_NOPE:]
    k_rope = jnp.broadcast_to(k_r[:, :, None, :], (b, t_len, MLA_HEADS, MLA_ROPE))
    k = jnp.concatenate([k_nope, k_rope], axis=-1)
    q = rmsnorm(q, q_head_norm)
    k = rmsnorm(k, k_head_norm)
    cos, sin = rope_tables(t_len)
    q = jnp.concatenate([q[..., :MLA_NOPE], apply_rope(q[..., MLA_NOPE:], cos, sin)], axis=-1)
    k = jnp.concatenate([k[..., :MLA_NOPE], apply_rope(k[..., MLA_NOPE:], cos, sin)], axis=-1)
    scale = MLA_QK ** -0.5
    n_real = t_len - N_META
    o_meta = dense_attend(q[:, :N_META], k, v, scale).reshape(b, N_META, MLA_WIDTH)
    q_blocks = jnp.moveaxis(q[:, N_META:].reshape(b, n_real // Q_BLOCK, Q_BLOCK, MLA_HEADS, MLA_QK), 1, 0)
    o_real = lax.map(lambda qb: dense_attend(qb, k, v, scale), q_blocks)
    o_real = jnp.moveaxis(o_real, 0, 1).reshape(b, n_real, MLA_WIDTH)
    return jnp.concatenate([o_meta, o_real], axis=1)

def na_mixer(q, k, v, q_head_norm, k_head_norm, rel_bias):
    b, t_len, _ = q.shape
    q = rmsnorm(q.reshape(b, t_len, NA_HEADS, NA_HEAD_DIM), q_head_norm)
    k = rmsnorm(k.reshape(b, t_len, NA_HEADS, NA_HEAD_DIM), k_head_norm)
    v = v.reshape(b, t_len, NA_HEADS, NA_HEAD_DIM)
    scale = NA_HEAD_DIM ** -0.5
    n_real = t_len - N_META
    rows = n_real // GRID_W
    kh = min(NA_MAX_ROWS, rows)
    q_m, k_m, v_m = q[:, :N_META], k[:, :N_META], v[:, :N_META]
    qg = q[:, N_META:].reshape(b, rows, GRID_W, NA_HEADS, NA_HEAD_DIM)
    kg = k[:, N_META:].reshape(b, rows, GRID_W, NA_HEADS, NA_HEAD_DIM)
    vg = v[:, N_META:].reshape(b, rows, GRID_W, NA_HEADS, NA_HEAD_DIM)
    col_start = np.clip(np.arange(GRID_W) - NA_KW // 2, 0, GRID_W - NA_KW)
    col_idx = col_start[:, None] + np.arange(NA_KW)[None, :]
    dc = col_idx - np.arange(GRID_W)[:, None] + (NA_KW - 1)
    bias_cols = rel_bias[:, :, dc]
    o_meta = dense_attend(q_m, k_m, v_m, scale).reshape(b, N_META, NA_WIDTH)

    def row_block(r):
        rs = jnp.clip(r - kh // 2, 0, rows - kh)
        q_row = lax.dynamic_index_in_dim(qg, r, axis=1, keepdims=False)
        k_win = lax.dynamic_slice_in_dim(kg, rs, kh, axis=1)[:, :, col_idx]
        v_win = lax.dynamic_slice_in_dim(vg, rs, kh, axis=1)[:, :, col_idx]
        dr = rs + jnp.arange(kh) - r + (NA_MAX_ROWS - 1)
        bias = jnp.transpose(bias_cols[:, dr], (0, 2, 1, 3)).reshape(NA_HEADS, GRID_W, kh * NA_KW)
        s_win = jnp.einsum('bchd,bicjhd->bhcij', q_row, k_win).reshape(b, NA_HEADS, GRID_W, kh * NA_KW)
        s_win = s_win.astype(jnp.float32) * scale + bias.astype(jnp.float32)[None]
        s_meta = jnp.einsum('bchd,bmhd->bhcm', q_row, k_m).astype(jnp.float32) * scale
        p = jax.nn.softmax(jnp.concatenate([s_meta, s_win], axis=-1), axis=-1).astype(v.dtype)
        p_meta = p[..., :N_META]
        p_win = p[..., N_META:].reshape(b, NA_HEADS, GRID_W, kh, NA_KW)
        return (jnp.einsum('bhcm,bmhd->bchd', p_meta, v_m)
                + jnp.einsum('bhcij,bicjhd->bchd', p_win, v_win))

    o_real = lax.map(row_block, jnp.arange(rows))
    o_real = jnp.moveaxis(o_real, 0, 1).reshape(b, n_real, NA_WIDTH)
    return jnp.concatenate([o_meta, o_real], axis=1)

def setup_inputs(seed: int = 0) -> dict:
    key = jax.random.key(seed)
    ks = jax.random.split(key, 24)

    def dense(k, shape, fan_in):
        return jax.random.normal(k, shape, jnp.float32) * fan_in ** -0.5

    def gain(k, shape):
        return 1.0 + 0.02 * jax.random.normal(k, shape, jnp.float32)

    L = DEPTH
    return {
        'x': jax.random.normal(ks[0], (BATCH, SEQ, D_MODEL), jnp.float32),
        'meta_tokens': jax.random.normal(ks[1], (N_META, D_MODEL), jnp.float32),
        'ffn1_norm': gain(ks[2], (L, D_MODEL)),
        'ffn1_w_gate': dense(ks[3], (L, D_MODEL, D_FF), D_MODEL),
        'ffn1_w_up': dense(ks[4], (L, D_MODEL, D_FF), D_MODEL),
        'ffn1_w_down': dense(ks[5], (L, D_FF, D_MODEL), D_FF),
        'mix_norm': gain(ks[6], (L, D_MODEL)),
        'w_in': dense(ks[7], (L, D_MODEL, IN_WIDTH), D_MODEL),
        'mla_q_a_norm': gain(ks[8], (L, Q_LORA)),
        'mla_w_uq': dense(ks[9], (L, Q_LORA, MLA_HEADS * MLA_QK), Q_LORA),
        'mla_kv_a_norm': gain(ks[10], (L, KV_LORA)),
        'mla_w_ukv': dense(ks[11], (L, KV_LORA, MLA_HEADS * (MLA_NOPE + MLA_V)), KV_LORA),
        'mla_q_head_norm': gain(ks[12], (L, MLA_QK)),
        'mla_k_head_norm': gain(ks[13], (L, MLA_QK)),
        'na_q_head_norm': gain(ks[14], (L, NA_HEAD_DIM)),
        'na_k_head_norm': gain(ks[15], (L, NA_HEAD_DIM)),
        'na_rel_bias': 0.02 * jax.random.normal(ks[16], (L, NA_HEADS, 2 * NA_MAX_ROWS - 1, 2 * NA_KW - 1), jnp.float32),
        'w_branch_a': dense(ks[17], (L, MLA_WIDTH, D_MODEL), MLA_WIDTH),
        'w_branch_b': dense(ks[18], (L, NA_WIDTH, D_MODEL), NA_WIDTH),
        'w_out': dense(ks[19], (L, D_MODEL, D_MODEL), D_MODEL),
        'ffn2_norm': gain(ks[20], (L, D_MODEL)),
        'ffn2_w_gate': dense(ks[21], (L, D_MODEL, D_FF), D_MODEL),
        'ffn2_w_up': dense(ks[22], (L, D_MODEL, D_FF), D_MODEL),
        'ffn2_w_down': dense(ks[23], (L, D_FF, D_MODEL), D_FF),
    }

def reference(x, meta_tokens, ffn1_norm, ffn1_w_gate, ffn1_w_up, ffn1_w_down, mix_norm, w_in,
              mla_q_a_norm, mla_w_uq, mla_kv_a_norm, mla_w_ukv, mla_q_head_norm, mla_k_head_norm,
              na_q_head_norm, na_k_head_norm, na_rel_bias, w_branch_a, w_branch_b, w_out,
              ffn2_norm, ffn2_w_gate, ffn2_w_up, ffn2_w_down):
    b = x.shape[0]
    split_points = np.cumsum(IN_SPLITS)[:-1].tolist()
    meta = jnp.broadcast_to(meta_tokens.astype(x.dtype)[None], (b, N_META, D_MODEL))
    h = jnp.concatenate([meta, x], axis=1)
    for l in range(DEPTH):
        h = h + 0.5 * swiglu(rmsnorm(h, ffn1_norm[l]), ffn1_w_gate[l], ffn1_w_up[l], ffn1_w_down[l])
        xn = rmsnorm(h, mix_norm[l])
        proj = xn @ w_in[l]
        c_q, c_kv, k_r, q_na, k_na, v_na, g_a, g_b = jnp.split(proj, split_points, axis=-1)
        o_a = mla_mixer(c_q, c_kv, k_r, mla_q_a_norm[l], mla_w_uq[l], mla_kv_a_norm[l], mla_w_ukv[l],
                        mla_q_head_norm[l], mla_k_head_norm[l])
        o_b = na_mixer(q_na, k_na, v_na, na_q_head_norm[l], na_k_head_norm[l], na_rel_bias[l])
        merged = jax.nn.sigmoid(g_a) * (o_a @ w_branch_a[l]) + jax.nn.sigmoid(g_b) * (o_b @ w_branch_b[l])
        h = h + merged @ w_out[l]
        h = h + 0.5 * swiglu(rmsnorm(h, ffn2_norm[l]), ffn2_w_gate[l], ffn2_w_up[l], ffn2_w_down[l])
    return h[:, N_META:]


_drawn_inputs = setup_inputs


def setup_inputs(seed=0):
    import zlib

    import numpy as np

    out = dict(_drawn_inputs(seed))
    spreads = {}
    factors = {'ffn1_norm': 6.468,
     'mix_norm': 8.0,
     'mla_q_a_norm': 8.0,
     'mla_kv_a_norm': 8.0,
     'mla_q_head_norm': 8.0,
     'mla_k_head_norm': 8.0,
     'na_q_head_norm': 8.0,
     'na_k_head_norm': 8.0,
     'na_rel_bias': 60.853,
     'ffn2_norm': 20.24}
    for name, (base, spread) in spreads.items():
        noise = np.random.default_rng([zlib.crc32(name.encode()), seed]).standard_normal(out[name].shape)
        drawn = base * np.exp(spread * noise) if base else spread * noise
        out[name] = __import__('jax').numpy.asarray(drawn.astype(out[name].dtype))
    for name, factor in factors.items():
        out[name] = (out[name] * factor).astype(out[name].dtype)
    return out
```

```python
from contextlib import ExitStack

import numpy as np

import concourse.bass as bass
from concourse import mybir

F32 = mybir.dt.float32
F32R = mybir.dt.float32r
BF16 = mybir.dt.bfloat16
ALU = mybir.AluOpType
ACT = mybir.ActivationFunctionType
AX = mybir.AxisListType

P = 128
D = 1024
DK = D // P
SEQ = 512
META = 16
T = SEQ + META
HALF = T // 2
FF = 2816
FC = FF // P
EPS = 1e-6
CONSTS = 5
PIECE = 1024
SLOTS = 3

HEADS = 8
PAIRS = HEADS // 2
QK = 96
NOPE = 64
ROPE = 32
HD = 64
QL = 384 // P
KL = 256 // P
ROWS = 8
BLK = 16
NEG = -1e30

G_FFN1, G_MIX, G_FFN2, G_QA, G_KVA, G_NAQ, G_NAK, G_MQ, G_MK = 0, 8, 16, 24, 27, 29, 30, 31, 32

C_FFN1 = 0
C_LAT = C_FFN1 + 3 * FC
C_NA = C_LAT + 6
C_UP = C_NA + 3 * PAIRS
C_GATE = C_UP + 5
C_OUT = C_GATE + 3 * DK
C_FFN2 = C_OUT + DK
N_PIECES = C_FFN2 + 3 * FC

ORDER = ("S0 T8p S1 T9p S2 PVp T0 S3 T1 S4 T2 S5 T3 S6 T4 S7 PV0 T5 S8 T6 S9 T7").split()
S_PAIR = {"S0": 0, "S1": 1, "S2": 0, "PVp": 1, "S3": 0, "S4": 1, "S5": 0, "S6": 1, "S7": 0, "PV0": 1,
          "S8": 0, "S9": 1}
UNITS = 10
NA_KEYS = ((0, 0), (0, 2), (0, 3), (1, 4), (2, 4))


def psum_pair(name):
    return S_PAIR[name] if name in S_PAIR else 2 + int(name[1]) % 2


def ds(start, n=1):
    return slice(start, start + n) if isinstance(start, int) else bass.ds(start, n)


def at_start(i):
    return isinstance(i, int) and i == 0


def att_job(j, name, i):
    if at_start(i):
        return j + 1 + sum(n[-1] != "p" for n in ORDER[:ORDER.index(name)])
    k = ORDER.index(name)
    if isinstance(i, int) and i == PAIRS:
        k = ("T8p", "T9p", "PVp").index(name)
    return j + len(ORDER) * i - 3 + k + 1


def att_prior(b, name, i):
    p = psum_pair(name)
    mine = [n for n in ORDER if psum_pair(n) == p]
    late = sum(n[-1] == "p" for n in mine)
    if at_start(i):
        return b[p] + sum(n[-1] != "p" for n in mine[:mine.index(name)])
    k = 0 if isinstance(i, int) and i == PAIRS else mine.index(name)
    return b[p] + len(mine) * i - late + k


def block_at(x):
    return (0, META) if x == 0 else (META + P * (x - 1), P)


class Own:

    def __init__(self, eng, semaphore):
        self.eng, self.semaphore = eng, semaphore
        self.base = self.n = self.per = self.i = 0

    def after(self, instruction):
        instruction.then_inc(self.semaphore, 1)
        self.n += 1
        self.eng.wait_ge(self.semaphore, self.base + self.n + (self.per * self.i if self.per else 0))

    def enter(self, per, i):
        self.base, self.n, self.per, self.i = self.base + self.n, 0, per, i

    def leave(self, steps):
        assert self.n == self.per, (self.n, self.per)
        self.base, self.n, self.per = self.base + self.per * steps, 0, 0


def build(nc, weights, xT, gains, mats, rope, mask, bias, out):
    n_pieces = weights.shape[0]
    assert n_pieces == N_PIECES
    with ExitStack() as ctx:
        def sb(name, shape, dt=F32):
            return ctx.enter_context(nc.sbuf_tensor(name, shape, dt))

        def sem(name):
            return ctx.enter_context(nc.semaphore(name))

        TILE = 4 * T
        place = [nc.sbuf_base + -nc.sbuf_base % 32]

        def take(size):
            place[0] += size
            return place[0] - size

        def at(name, byte, shape, dt=F32):
            return nc.alloc_sbuf_tensor_at(name, shape, dt, offset=byte)

        h = at("h", take(8 * TILE), [P, DK, T])
        x_hi = at("x_hi", take(8 * TILE), [P, DK, T], F32R)
        x_lo = at("x_lo", take(8 * TILE), [P, DK, T], F32R)
        w_raw = at("w_raw", take(4 * SLOTS * PIECE), [P, SLOTS, PIECE])
        w_hi = at("w_hi", take(4 * SLOTS * PIECE), [P, SLOTS, PIECE], F32R)
        w_lo = at("w_lo", take(4 * SLOTS * PIECE), [P, SLOTS, PIECE], F32R)
        gain = at("gain", take(160), [P, gains.shape[1]])
        mat = at("mat", take(12 * P), [P, 3, P])
        ones = at("ones", take(4 * P), [P, P])
        eps = at("eps", take(32), [P, 3])
        q_scale = at("q_scale", take(160), [P, 5, HEADS])
        q_scale2 = at("q_scale2", take(64), [P, 5, 2])
        neg_max = at("neg_max", take(64), [P, UNITS])
        exp_bias = at("exp_bias", take(64), [P, UNITS])
        exp_sum = at("exp_sum", take(64), [P, UNITS])
        exp_rec = at("exp_rec", take(64), [P, UNITS])

        hid_at = take(2 * TILE)
        hid_hi = at("hid_hi", hid_at, [P, T], F32R)
        hid_lo = at("hid_lo", hid_at + TILE, [P, T], F32R)
        rot_k = at("rot_k", hid_at, [P, T])
        rot_sq = at("rot_sq", hid_at + TILE, [P, T])

        scratch = take(6 * TILE)
        silu = at("silu", scratch, [P, T])
        hid = at("hid", scratch + TILE, [P, T])
        sq = at("sq", scratch + 2 * TILE, [P, 2, T])
        xs = at("xs", scratch + 4 * TILE, [P, 2, T])
        prob = at("prob", scratch, [P, 5, T])
        gate_a = at("gate_a", scratch, [P, T])
        gate_b = at("gate_b", scratch + TILE, [P, T])
        part_a = at("part_a", scratch + 2 * TILE, [P, T])
        part_b = at("part_b", scratch + 3 * TILE, [P, T])
        merged = at("merged", scratch + 4 * TILE, [P, T])
        rms = at("rms", take(TILE), [P, T])
        rstd = at("rstd", take(TILE), [P, T])

        MASK_W = sum(P * (b - a) for a, b in (NA_KEYS[1], NA_KEYS[2], NA_KEYS[4]))
        late = take(2 * TILE + 2 * MASK_W + 8 * (MASK_W + 3 * META))
        cos = at("cos", late, [P, T])
        sin = at("sin", late + TILE, [P, T])
        na_mask = at("na_mask", late + 2 * TILE, [P, MASK_W], BF16)
        na_bias = at("na_bias", late + 2 * TILE + 2 * MASK_W, [P, 2, MASK_W + 3 * META])

        mix = place[0]
        v_at, pt_at = mix + 8 * TILE, mix + 8 * TILE + 20 * 4 * P
        vs_at = pt_at + 10 * TILE
        o_at = vs_at + 10 * 4 * P
        end = o_at + 16 * TILE
        assert end <= nc.sbuf_usable_end
        val = at("val", v_at, [P, 5, 4 * P])
        p_hi = at("p_hi", pt_at, [P, 5, T], F32R)
        p_lo = at("p_lo", pt_at + 5 * TILE, [P, 5, T], F32R)
        v_hi = at("v_hi", vs_at, [P, 5, P], F32R)
        v_lo = at("v_lo", vs_at + 20 * P, [P, 5, P], F32R)
        o = at("o", o_at, [P, 8, T])
        na_q = at("na_q", mix, [P, PAIRS, T])
        na_k = at("na_k", mix + 4 * TILE, [P, PAIRS, T])
        lat = at("lat", o_at + 4 * TILE, [P, QL + KL, T])
        lat_sq = at("lat_sq", pt_at, [P, QL + KL, T])
        lat_hi = at("lat_hi", pt_at, [P, QL + KL, T], F32R)
        lat_lo = at("lat_lo", pt_at + 5 * TILE, [P, QL + KL, T], F32R)
        na_s = [at(f"na_{n}", o_at + (9 + k) * TILE, [P, T], F32R)
                for k, n in enumerate(("q_hi", "q_lo", "k_hi", "k_lo"))]
        raw_bias = at("raw_bias", o_at + 13 * TILE, [P, 3 * P])
        m_q = at("m_q", mix, [P, HEADS, T])
        m_k = at("m_k", o_at + 8 * TILE, [P, HEADS, T])
        m_s = [[at(f"m_{n}{e}", b, [P, T], F32R) for n, b in zip(("q_hi", "q_lo", "k_hi", "k_lo"), where)]
               for e, where in enumerate((
                   [late, late + TILE, late + 2 * TILE, late + 3 * TILE],
                   [late + 4 * TILE, late + 5 * TILE, hid_at, hid_at + TILE]))]
        o_hi = at("o_hi", mix, [P, 8, T], F32R)
        o_lo = at("o_lo", mix + 8 * TILE, [P, 8, T], F32R)
        g_hi = at("g_hi", mix + 16 * TILE, [P, DK, T], F32R)
        g_lo = at("g_lo", mix + 24 * TILE, [P, DK, T], F32R)

        ps = ctx.enter_context(nc.psum_tensor("ps", [P, 8, 512], F32))

        load_x = [sem(f"load_x{m}") for m in range(DK)]
        load_c = sem("load_c")
        loaded = [sem(f"w_loaded{s}") for s in range(SLOTS)]
        hi_done = sem("w_hi_done")
        lo_done = sem("w_lo_done")
        jobs = sem("pe_jobs")
        free = [sem(f"psum_free{p}") for p in range(4)]
        const_ready = sem("const_ready")
        stored = sem("stored")
        sq_ready = sem("sq_ready")
        sq_used = sem("sq_used")
        rstd_ready = sem("rstd_ready")
        xs_ready = sem("xs_ready")
        x_hi_done = sem("x_hi_done")
        x_split = sem("x_split")
        hid_hi_done = sem("hid_hi_done")
        pool_ready = sem("pool_ready")
        small_turn = sem("small_turn")
        dve_own = sem("dve_own")
        lat_hi_done = sem("lat_hi_done")
        lat_split = sem("lat_split")
        rms_read = sem("rms_read")
        na_k_ready = sem("na_k_ready")
        rot_ready = sem("rot_ready")
        m_stat_read = sem("m_stat_read")
        m_done = sem("m_done")
        o_hi_done = sem("o_hi_done")
        o_split = sem("o_split")
        g_ready = sem("g_ready")
        g_hi_done = sem("g_hi_done")
        g_split = sem("g_split")
        bias_loaded = sem("bias_loaded")
        bias_ready = sem("bias_ready")
        hid_split = sem("hid_split")

        def pair(p):
            return ps[:, 2 * p:2 * p + 2, 0:HALF]

        def two(ap):
            return ap.rearrange("p (a c) -> p a c", a=2)

        dve = Own(nc.vector, dve_own)

        def wait(eng, semaphore, value):
            if not isinstance(value, int) or value > 0:
                eng.wait_ge(semaphore, value)

        def split_hi(c, i, left):
            s = c % SLOTS
            nc.scalar.wait_ge(loaded[s], 16 * (c // SLOTS + 1 + i))
            wait(nc.scalar, jobs, left)
            nc.scalar.activation(w_hi[:, s, :], w_raw[:, s, :], ACT.Copy).then_inc(hi_done, 1)

        def split_lo(c, i):
            s = c % SLOTS
            nc.vector.wait_ge(hi_done, c + 1 + 3 * i)
            nc.vector.tensor_tensor(w_lo[:, s, :], w_raw[:, s, :], w_hi[:, s, :],
                                    ALU.subtract).then_inc(lo_done, 1)

        def weight(c, k, width=P):
            s = c % SLOTS
            return w_hi[:, s, k * width:(k + 1) * width], w_lo[:, s, k * width:(k + 1) * width]

        def three_passes(dst, w, r, first, last, rows=P):
            for n, (x, y) in enumerate(((w[0], r[0]), (w[0], r[1]), (w[1], r[0]))):
                for a in range(2):
                    mm = nc.tensor.matmul(dst[0:rows, a, :], x, y[:, a * HALF:(a + 1) * HALF],
                                          start=first and n == 0, stop=last and n == 2)
            return mm

        def x_tile(k):
            return x_hi[:, k, :], x_lo[:, k, :]

        def act_norm_squares(v, p, job, h_ready):
            for m in range(DK):
                nc.scalar.wait_ge(*h_ready[m])
                if m >= 2:
                    nc.scalar.wait_ge(sq_used, (DK - 1) * v + m - 1)
                nc.scalar.activation(sq[:, m % 2, :], h[:, m, :], ACT.Square).then_inc(sq_ready, 1)
            nc.scalar.wait_ge(jobs, job)
            wait(nc.scalar, rstd_ready, v)
            nc.scalar.activation(two(rms[:]), pair(p), ACT.Sqrt, bias=eps[:, 0:1],
                                 scale=1.0 / D).then_inc(free[p], 1)

        def pe_norm_sums(v, p, prior):
            wait(nc.tensor, free[p], prior)
            for m in range(DK):
                nc.tensor.wait_ge(sq_ready, DK * v + m + 1)
                for a in range(2):
                    mm = nc.tensor.matmul(pair(p)[:, a, :], ones[:], sq[:, m % 2, a * HALF:(a + 1) * HALF],
                                          start=m == 0, stop=m == DK - 1)
                mm.then_inc(jobs if m == DK - 1 else sq_used, 1)

        def act_norm_hi(v):
            for m in range(DK):
                nc.scalar.wait_ge(xs_ready, DK * v + m + 1)
                nc.scalar.activation(x_hi[:, m, :], xs[:, m % 2, :], ACT.Copy).then_inc(x_hi_done, 1)

        def dve_norm(v, p, prior, g0):
            nc.vector.wait_ge(free[p], prior + 1)
            nc.vector.reciprocal(rstd[:], rms[:]).then_inc(rstd_ready, 1)
            nc.vector.wait_ge(rstd_ready, v + 1)
            for m in range(DK + 1):
                if m < DK:
                    wait(nc.vector, x_split, DK * v + m - 1)
                    nc.vector.scalar_tensor_tensor(xs[:, m % 2, :], h[:, m, :], gain[:, g0 + m:g0 + m + 1],
                                                   rstd[:], ALU.mult, ALU.mult).then_inc(xs_ready, 1)
                if m > 0:
                    nc.vector.wait_ge(x_hi_done, DK * v + m)
                    nc.vector.tensor_tensor(x_lo[:, m - 1, :], xs[:, (m - 1) % 2, :], x_hi[:, m - 1, :],
                                            ALU.subtract).then_inc(x_split, 1)

        DOWN_PAIR = (2, 3, 0, 1, 2, 3, 2, 3)

        def up_prior(b, p, i):
            return b[p] if isinstance(i, int) and i == 0 else b[p] + 2 * i - 1

        def down_prior(b, m, i):
            p = DOWN_PAIR[m]
            if p < 2:
                return b[p] + 2 * i - (1 if isinstance(i, int) and i == FC else 0)
            return b[p] + 3 * i - 3 + (0, 0, 0, 0, 1, 1, 2, 2)[m]

        def up_job(j, which, i):
            return j + 1 + which if isinstance(i, int) and i == 0 else j + 10 * i - 7 + which

        def down_tile_job(j, m, i):
            return j + 10 * i - (7 if isinstance(i, int) and i == FC else 5) + m

        def after_ffn(b, j):
            return [b[0] + 2 * FC, b[1] + 2 * FC, b[2] + 3 * FC, b[3] + 3 * FC], j + 10 * FC

        def pe_ffn(f, v, c, b):
            def up(p, cc, ii, i):
                nc.tensor.wait_ge(lo_done, cc + 1 + 3 * ii)
                wait(nc.tensor, free[p], up_prior(b, p, i))
                for k in range(DK):
                    if isinstance(i, int) and i == 0 and p == 0:
                        nc.tensor.wait_ge(x_split, DK * v + k + 1)
                    mm = three_passes(pair(p), weight(cc, k), x_tile(k), k == 0, k == DK - 1)
                mm.then_inc(jobs, 1)

            def down(cc, ii, i):
                nc.tensor.wait_ge(lo_done, cc + 1 + 3 * ii)
                nc.tensor.wait_ge(hid_split, FC * f + i)
                for m in range(DK):
                    p = DOWN_PAIR[m]
                    wait(nc.tensor, free[p], down_prior(b, m, i))
                    three_passes(pair(p), weight(cc, m), (hid_hi[:], hid_lo[:]), True, True).then_inc(jobs, 1)

            def step(i):
                up(0, c - 1, i, i)
                up(1, c, i, i)
                down(c + 1, i, i)

            up(0, c, 0, 0)
            up(1, c + 1, 0, 0)
            step(1)
            with nc.tensor.Fori(2, FC) as i:
                step(i)
            down(c + 3 * FC - 1, 0, FC)

        def act_ffn(c, b, j, f):
            def gate(i):
                nc.scalar.wait_ge(jobs, up_job(j, 0, i))
                if not (isinstance(i, int) and i == 0):
                    nc.scalar.wait_ge(free[1], up_prior(b, 1, i - 1) + 1)
                nc.scalar.activation(two(silu[:]), pair(0), ACT.Silu).then_inc(free[0], 1)

            def hidden(i):
                nc.scalar.wait_ge(free[1], up_prior(b, 1, i) + 1)
                if not (isinstance(i, int) and i == 0):
                    nc.scalar.wait_ge(jobs, down_tile_job(j, DK - 1, i))
                nc.scalar.activation(hid_hi[:], hid[:], ACT.Copy).then_inc(hid_hi_done, 1)

            def step(i):
                split_hi(c + 1, i, down_tile_job(j, DK - 1, i - 1) if not (isinstance(i, int) and i == 1)
                         else up_job(j, 1, 0))
                gate(i)
                split_hi(c + 2, i, up_job(j, 0, i))
                if not (isinstance(i, int) and i == FC - 1 and c + 3 * FC >= n_pieces):
                    split_hi(c + 3, i, up_job(j, 1, i))
                hidden(i)

            gate(0)
            split_hi(c + 3, 0, up_job(j, 0, 0))
            hidden(0)
            step(1)
            with nc.scalar.Fori(2, FC - 1) as i:
                step(i)
            step(FC - 1)

        def dve_ffn(c, b, j, f):
            def up(i):
                nc.vector.wait_ge(jobs, up_job(j, 1, i))
                nc.vector.wait_ge(free[0], up_prior(b, 0, i) + 1)
                wait(nc.vector, hid_split, FC * f + i)
                nc.vector.tensor_tensor(two(hid[:]), pair(1), two(silu[:]), ALU.mult).then_inc(free[1], 1)

            def down(i):
                for m in range(DK):
                    nc.vector.wait_ge(jobs, down_tile_job(j, m, i))
                    nc.vector.scalar_tensor_tensor(two(h[:, m, :]), pair(DOWN_PAIR[m]), 0.5, two(h[:, m, :]),
                                                   ALU.mult, ALU.add).then_inc(free[DOWN_PAIR[m]], 1)

            def step(i):
                split_lo(c + 1, i)
                split_lo(c + 2, i)
                up(i)
                down(i)
                if not (isinstance(i, int) and i == FC - 1 and c + 3 * FC >= n_pieces):
                    split_lo(c + 3, i)

            up(0)
            split_lo(c + 3, 0)
            step(1)
            with nc.vector.Fori(2, FC - 1) as i:
                step(i)
            step(FC - 1)
            down(FC)

        def pool_ffn(f):
            with nc.gpsimd.Fori(0, FC) as i:
                nc.gpsimd.wait_ge(hid_hi_done, FC * f + 1 + i)
                nc.gpsimd.tensor_tensor(hid_lo[:], hid[:], hid_hi[:], ALU.subtract).then_inc(hid_split, 1)

        def ffn_h_ready(b):
            return [(free[DOWN_PAIR[m]], down_prior(b, m, FC) + 1) for m in range(DK)]

        def pe_latents(j, b):
            for k in range(6):
                c, p = C_LAT + k, k % 4
                nc.tensor.wait_ge(lo_done, c + 1)
                wait(nc.tensor, free[p], b[p] + k // 4)
                for t in range(DK):
                    if k == 0:
                        nc.tensor.wait_ge(x_split, DK + t + 1)
                    mm = three_passes(pair(p), weight(c, t), x_tile(t), t == 0, t == DK - 1)
                mm.then_inc(jobs, 1)
            for p, tiles, (last, prior) in ((2, range(QL), (3, b[3] + 1)), (3, range(QL, QL + KL), (1, b[1] + 2))):
                nc.tensor.wait_ge(free[last], prior)
                nc.tensor.wait_ge(free[p], b[p] + 1)
                for t in tiles:
                    for a in range(2):
                        mm = nc.tensor.matmul(pair(p)[:, a, :], ones[:], lat_sq[:, t, a * HALF:(a + 1) * HALF],
                                              start=t == tiles[0], stop=t == tiles[-1])
                mm.then_inc(jobs, 1)

        def act_latents(j, b):
            for k in range(6):
                p = k % 4
                nc.scalar.wait_ge(jobs, j + 1 + k)
                if k == 0:
                    nc.scalar.activation(two(rot_k[NOPE:QK, :]), pair(p)[NOPE:QK], ACT.Copy,
                                         scale=gain[NOPE:QK, G_MK:G_MK + 1])
                    nc.scalar.activation(two(rot_sq[NOPE:QK, :]), pair(p)[NOPE:QK], ACT.Square).then_inc(free[p], 1)
                else:
                    nc.scalar.activation(two(lat[:, k - 1, :]), pair(p), ACT.Copy)
                    nc.scalar.activation(two(lat_sq[:, k - 1, :]), pair(p), ACT.Square).then_inc(free[p], 1)
                split_hi(C_LAT + 3 + k, 0, j + 1 + k)
            for k, (p, width) in enumerate(((2, QL * P), (3, KL * P))):
                nc.scalar.wait_ge(jobs, j + 7 + k)
                nc.scalar.wait_ge(rms_read, k) if k else nc.scalar.wait_ge(rstd_ready, 2)
                nc.scalar.activation(two(rms[:]), pair(p), ACT.Sqrt, bias=eps[:, 0:1],
                                     scale=1.0 / width).then_inc(free[p], 1)

        def dve_latents(j, b):
            for k in range(6):
                split_lo(C_LAT + 3 + k, 0)
            for k, (p, g, tiles) in enumerate(((2, G_QA, range(QL)), (3, G_KVA, range(QL, QL + KL)))):
                nc.vector.wait_ge(free[p], b[p] + 2)
                nc.vector.reciprocal(rstd[:], rms[:]).then_inc(rms_read, 1)
                nc.vector.wait_ge(rms_read, k + 1)
                for t in tiles:
                    col = g + t - tiles[0]
                    ins = nc.vector.scalar_tensor_tensor(lat[:, t, :], lat[:, t, :], gain[:, col:col + 1], rstd[:],
                                                         ALU.mult, ALU.mult)
                dve.after(ins)

        STAT = 272

        def pe_na_heads(j, b):
            with nc.tensor.Fori(0, PAIRS) as i:
                for p in range(3):
                    c = C_NA + p
                    nc.tensor.wait_ge(lo_done, c + 1 + 3 * i)
                    nc.tensor.wait_ge(free[p], b[p] + i)
                    if p < 2:
                        for t in range(DK):
                            mm = three_passes(pair(p), weight(c, t), x_tile(t), t == 0, t == DK - 1)
                    else:
                        for x in range(5):
                            q0, n = block_at(x)
                            dst = ps[0:n, 2 * p + (x == 0), P * max(x - 1, 0):P * max(x, 1)]
                            for t in range(DK):
                                w, r = weight(c, t), x_tile(t)
                                for k, (l, m) in enumerate(((r[0], w[0]), (r[1], w[0]), (r[0], w[1]))):
                                    mm = nc.tensor.matmul(dst, l[:, q0:q0 + n], m, start=t == 0 and k == 0,
                                                          stop=t == DK - 1 and k == 2)
                    mm.then_inc(jobs, 1)
                nc.tensor.wait_ge(free[0], b[0] + 1 + i)
                nc.tensor.wait_ge(free[1], b[1] + 1 + i)
                nc.tensor.wait_ge(free[3], b[3] + i)
                for x in range(5):
                    q0, n = block_at(x)
                    nc.tensor.matmul(ps[0:n, 6, STAT + 2 * x:STAT + 2 * x + 2], sq[:, 0, q0:q0 + n],
                                     mat[:, 1, 0:P:HD], start=True, stop=True)
                for a in range(2):
                    mm = nc.tensor.matmul(pair(3)[:, a, :], mat[:, 1, :], sq[:, 1, a * HALF:(a + 1) * HALF],
                                          start=True, stop=True)
                mm.then_inc(jobs, 1)

        def act_na_heads(j, b):
            with nc.scalar.Fori(0, PAIRS) as i:
                for p, (dst, g) in enumerate(((na_q, G_NAQ), (na_k, G_NAK))):
                    nc.scalar.wait_ge(jobs, j + 1 + p + 4 * i)
                    nc.scalar.activation(two(dst[:, ds(i), :].rearrange("p a t -> p (a t)")), pair(p), ACT.Copy,
                                         scale=gain[:, g:g + 1])
                    nc.scalar.activation(two(sq[:, p, :]), pair(p), ACT.Square).then_inc(free[p], 1)
                    split_hi(C_NA + 3 + p, i, j + 1 + p + 4 * i)
                nc.scalar.wait_ge(jobs, j + 3 + 4 * i)
                nc.scalar.activation(val[:, 1:5, ds(P * i, P)], ps[:, 4, :].rearrange("p (x f) -> p x f", f=P), ACT.Copy)
                nc.scalar.activation(val[0:META, 0, ds(P * i, P)], ps[0:META, 5, 0:P], ACT.Copy).then_inc(free[2], 1)
                split_hi(C_NA + 5, i, j + 3 + 4 * i)
                nc.scalar.wait_ge(jobs, j + 4 + 4 * i)
                nc.scalar.activation(q_scale[:, 1:5, ds(2 * i, 2)],
                                     ps[:, 6, STAT + 2:STAT + 10].rearrange("p (x e) -> p x e", e=2),
                                     ACT.Sqrt, bias=eps[:, 1:2])
                nc.scalar.activation(q_scale[0:META, 0, ds(2 * i, 2)], ps[0:META, 6, STAT:STAT + 2],
                                     ACT.Sqrt, bias=eps[0:META, 1:2])
                nc.scalar.wait_ge(rms_read, 2 + i)
                nc.scalar.activation(two(rms[:]), pair(3), ACT.Sqrt, bias=eps[:, 0:1],
                                     scale=1.0 / HD).then_inc(free[3], 1)

        def dve_na_heads(j, b):
            with nc.vector.Fori(0, PAIRS) as i:
                for k in range(3):
                    split_lo(C_NA + 3 + k, i)
                nc.vector.wait_ge(free[3], b[3] + 1 + i)
                nc.vector.reciprocal(rstd[:], rms[:]).then_inc(rms_read, 1)
                nc.vector.wait_ge(rms_read, 3 + i)
                k_i = na_k[:, ds(i), :].rearrange("p a t -> p (a t)")
                nc.vector.tensor_tensor(k_i, k_i, rstd[:], ALU.mult).then_inc(na_k_ready, 1)
                nc.vector.wait_ge(na_k_ready, i + 1)
            dve.after(nc.vector.reciprocal(q_scale[:], q_scale[:]))

        class Sync:

            def __init__(self, name):
                self.q_hi, self.q_lo = sem(f"{name}_split_hi"), sem(f"{name}_split_lo")
                self.bias = sem(f"{name}_exp_bias")
                self.exp = sem(f"{name}_exp")
                self.prob = sem(f"{name}_prob")
                self.p_hi = sem(f"{name}_p_hi")
                self.scale = sem(f"{name}_scale")

        na_sync, m_sync = Sync("na"), Sync("mla")

        def steps(eng, body):
            body(0)
            with eng.Fori(1, PAIRS) as i:
                body(i)

        def na_width(x):
            a, e = NA_KEYS[x]
            return META + P * (e - a)

        def splits_per_step(mla):
            return 5 if mla else 3

        def scores_at(mla, x, p):
            return pair(p)[0:block_at(x)[1]] if mla else ps[0:block_at(x)[1], 2 * p, 0:na_width(x)]

        def prob_at(mla, u, x):
            n = block_at(x)[1]
            return two(prob[0:n, u % 5, :]) if mla else prob[0:n, u % 5, 0:na_width(x)]

        def pe_attention(mla, y, j, b):
            def scores(u, i):
                e, x = divmod(u, 5)
                q0, n = block_at(x)
                p = S_PAIR[f"S{u}"]
                wait(nc.tensor, free[p], att_prior(b, f"S{u}", i))
                if mla and x == 0:
                    nc.tensor.wait_ge(y.q_lo, 2 + 2 * e + 5 * i)
                elif u == 0:
                    nc.tensor.wait_ge(y.q_lo, 2 + 3 * i)
                if x == 0:
                    nc.tensor.sem_inc(small_turn, 1)
                qh, ql, kh, kl = m_s[e] if mla else na_s
                rows = slice(0, QK) if mla else slice(HD * e, HD * e + HD)
                if mla:
                    parts = [(pair(p)[0:n, a, :], a * HALF, HALF) for a in range(2)]
                else:
                    a, z = NA_KEYS[x]
                    parts = [(ps[0:n, 2 * p, 0:META], 0, META)]
                    if x:
                        parts.append((ps[0:n, 2 * p, META:na_width(x)], META + P * a, P * (z - a)))
                for dst, k0, w in parts:
                    for k, (l, r) in enumerate(((qh, kh), (qh, kl), (ql, kh))):
                        mm = nc.tensor.matmul(dst, l[rows, q0:q0 + n], r[rows, k0:k0 + w], start=k == 0, stop=k == 2)
                mm.then_inc(jobs, 1)

            def transposes(name, i, step):
                u = int(name[1])
                x = u % 5
                n, p = block_at(x)[1], 2 + u % 2
                nc.tensor.wait_ge(y.prob, UNITS * step + u + 1)
                wait(nc.tensor, free[p], att_prior(b, name, i))
                if x == 0:
                    nc.tensor.sem_inc(small_turn, 1)
                a, z = (0, 4) if mla else NA_KEYS[x]
                src = prob[0:n, u % 5, :]
                for k in range(z - a):
                    nc.tensor.transpose(ps[:, 2 * p, P * k:P * k + n], src[:, META + P * k:META + P * (k + 1)],
                                        mat[0:n, 0, 0:n])
                nc.tensor.transpose(ps[0:META, 2 * p + 1, 0:n], src[:, 0:META], mat[0:n, 0, 0:n]).then_inc(jobs, 1)

            def values(name, i, step):
                e = 1 if name == "PVp" else 0
                last = "T9p" if e else "T4"
                nc.tensor.wait_ge(free[psum_pair(last)], att_prior(b, last, i) + 1)
                wait(nc.tensor, free[1], att_prior(b, name, i))
                if not e:
                    nc.tensor.wait_ge(y.q_lo, splits_per_step(mla) * (i + 1))
                m = P if e else HD
                if mla:
                    groups = [(2, 0, 272, [(a, 0, 272) for a in range(5)]),
                              (3, 272, 256, [(a, 272, 256) for a in range(5)])]
                else:
                    groups = [(2, META, SEQ, [(0, META, SEQ)] + [
                        (1 + a, META + P * lo, P * (hi - lo)) for a, (lo, hi) in enumerate(NA_KEYS[1:])]),
                        (3, 0, META, [(0, 0, META)])]
                for bank, base, _, parts in groups:
                    for k, (a, q0, w) in enumerate(parts):
                        rows = slice(0, META if a == 0 else P)
                        for t, (l, r) in enumerate(((v_hi, p_hi), (v_hi, p_lo), (v_lo, p_hi))):
                            mm = nc.tensor.matmul(ps[0:m, bank, q0 - base:q0 - base + w], l[rows, a, 0:m],
                                                  r[rows, a, q0:q0 + w], start=k == 0 and t == 0,
                                                  stop=k == len(parts) - 1 and t == 2)
                mm.then_inc(jobs, 1)

            def step(i):
                for name in ORDER:
                    late_one = name[-1] == "p"
                    if late_one and at_start(i):
                        continue
                    before = i - 1 if late_one else i
                    if name[0] == "S":
                        scores(int(name[1]), i)
                    elif name[0] == "T":
                        transposes(name, i, before)
                    else:
                        values(name, i, before)

            steps(nc.tensor, step)
            for name in ("T8p", "T9p"):
                transposes(name, PAIRS, PAIRS - 1)
            values("PVp", PAIRS, PAIRS - 1)

        def split_q_k(mla, e, i):
            if mla:
                return [(m_q[0:QK, ds(2 * i + e), :].rearrange("p a t -> p (a t)"), m_s[e][0][0:QK], m_s[e][1][0:QK]),
                        (m_k[0:QK, ds(2 * i + e), :].rearrange("p a t -> p (a t)"), m_s[e][2][0:QK], m_s[e][3][0:QK])]
            return [(na_q[:, ds(i), :].rearrange("p a t -> p (a t)"), na_s[0][:], na_s[1][:]),
                    (na_k[:, ds(i), :].rearrange("p a t -> p (a t)"), na_s[2][:], na_s[3][:])]

        def act_attention(mla, y, j, b):
            def split(e, i):
                if not at_start(i):
                    nc.scalar.wait_ge(jobs, att_job(j, "S4" if mla and e == 0 else "S9", i - 1))
                if not mla:
                    nc.scalar.wait_ge(na_k_ready, i + 1)
                elif e == 0 and at_start(i):
                    nc.scalar.wait_ge(m_done, 2 * HEADS)
                for src, hi, _ in split_q_k(mla, e, i):
                    nc.scalar.activation(hi, src, ACT.Copy).then_inc(y.q_hi, 1)

            def exp(u, i):
                e, x = divmod(u, 5)
                n = block_at(x)[1]
                p = S_PAIR[f"S{u}"]
                nc.scalar.wait_ge(y.bias, UNITS * i + u + 1)
                if mla:
                    if u >= 5 or not at_start(i):
                        nc.scalar.wait_ge(jobs, att_job(j, *buffer_user(u, i)))
                    nc.scalar.activation(prob_at(mla, u, x), scores_at(mla, x, p), ACT.Exp,
                                         bias=exp_bias[0:n, u:u + 1], scale=q_scale2[0:n, x, e:e + 1],
                                         accum_out=exp_sum[0:n, u:u + 1]).then_inc(free[p], 1)
                else:
                    nc.scalar.activation(prob_at(mla, u, x), prob_at(mla, u, x), ACT.Exp, bias=neg_max[0:n, u:u + 1],
                                         accum_out=exp_sum[0:n, u:u + 1]).then_inc(y.exp, 1)

            def hi_of_transposed(name, i, step):
                u = int(name[1])
                x = u % 5
                (q0, n), p = block_at(x), 2 + u % 2
                nc.scalar.wait_ge(jobs, att_job(j, name, i))
                a, z = (0, 4) if mla else NA_KEYS[x]
                if z > a:
                    nc.scalar.activation(p_hi[:, 1 + a:1 + z, q0:q0 + n], blocks(p, z - a, n), ACT.Copy)
                nc.scalar.activation(p_hi[0:META, 0, q0:q0 + n], ps[0:META, 2 * p + 1, 0:n],
                                     ACT.Copy).then_inc(y.p_hi, 1)

            def output(name, i, pair_no):
                e = 1 if name == "PVp" else 0
                rows = slice(HD * e, HD * e + HD)
                nc.scalar.wait_ge(jobs, att_job(j, name, i))
                t = pair_no + 4 if mla else pair_no
                cuts = ((2, 0, 272), (3, 272, 256)) if mla else ((2, META, SEQ), (3, 0, META))
                for k, (bank, q0, w) in enumerate(cuts):
                    ins = nc.scalar.activation(o[rows, ds(t), q0:q0 + w].rearrange("p a t -> p (a t)"),
                                               ps[rows, bank, 0:w], ACT.Copy)
                ins.then_inc(free[1], 1)

            def step(i):
                split(0, i)
                for u in range(UNITS):
                    if mla and u == 2:
                        split(1, i)
                    if u == 3:
                        if not at_start(i):
                            nc.scalar.wait_ge(jobs, att_job(j, "PVp", i))
                        nc.scalar.activation(v_hi[:], val[:, :, ds(P * i, P)], ACT.Copy).then_inc(y.q_hi, 1)
                    exp(u, i)
                    if u == 2 and not at_start(i):
                        output("PVp", i, i - 1)
                    if u == 7:
                        output("PV0", i, i)
                    if u >= 2:
                        hi_of_transposed(f"T{u - 2}", i, i)
                    elif not at_start(i):
                        hi_of_transposed(f"T{u + 8}p", i, i - 1)

            steps(nc.scalar, step)
            hi_of_transposed("T8p", PAIRS, PAIRS - 1)
            hi_of_transposed("T9p", PAIRS, PAIRS - 1)
            output("PVp", PAIRS, PAIRS - 1)

        def buffer_user(u, i):
            if u >= 5:
                return f"T{u - 5}", i
            return (f"T{u + 5}", i - 1) if u < 3 else (f"T{u + 5}p", i)

        def blocks(p, count, n):
            return ps[:, 2 * p, 0:P * count].rearrange("p (k q) -> p k q", q=P)[:, :, 0:n]

        def dve_attention(mla, y, j, b):
            def split(e, i):
                first = splits_per_step(mla) * i + 2 * e
                for k, (src, hi, lo) in enumerate(split_q_k(mla, e, i)):
                    nc.vector.wait_ge(y.q_hi, first + k + 1)
                    nc.vector.tensor_tensor(lo, src, hi, ALU.subtract).then_inc(y.q_lo, 1)

            def top(u, i):
                e, x = divmod(u, 5)
                n = block_at(x)[1]
                p = S_PAIR[f"S{u}"]
                nc.vector.wait_ge(jobs, att_job(j, f"S{u}", i))
                if mla:
                    dve.after(nc.vector.tensor_reduce(neg_max[0:n, u:u + 1], scores_at(mla, x, p), AX.XY, ALU.max,
                                                      negate=True))
                    nc.vector.tensor_tensor(exp_bias[0:n, u:u + 1], neg_max[0:n, u:u + 1],
                                            q_scale2[0:n, x, e:e + 1], ALU.mult).then_inc(y.bias, 1)
                    return
                if u >= 5 or not at_start(i):
                    nc.vector.wait_ge(jobs, att_job(j, *buffer_user(u, i)))
                w = na_width(x)
                if x == 0:
                    nc.vector.tensor_scalar(prob[0:n, u % 5, 0:w], ps[0:n, 2 * p, 0:w], q_scale2[0:n, x, e:e + 1],
                                            None, ALU.mult).then_inc(free[p], 1)
                else:
                    if x == 1:
                        nc.vector.wait_ge(bias_ready, 3 * (2 * i + e) + 3)
                    at_bias = (0, 0, META + 2 * P, META + 2 * P, 2 * META + 5 * P)[x]
                    nc.vector.scalar_tensor_tensor(prob[:, u % 5, 0:w], ps[:, 2 * p, 0:w], q_scale2[:, x, e:e + 1],
                                                   na_bias[:, e, at_bias:at_bias + w], ALU.mult,
                                                   ALU.add).then_inc(free[p], 1)
                nc.vector.wait_ge(free[p], att_prior(b, f"S{u}", i) + 1)
                nc.vector.tensor_reduce(neg_max[0:n, u:u + 1], prob[0:n, u % 5, 0:w], AX.X, ALU.max,
                                        negate=True).then_inc(y.bias, 1)

            def normalise(u, i):
                x = u % 5
                n = block_at(x)[1]
                if mla:
                    nc.vector.wait_ge(free[S_PAIR[f"S{u}"]], att_prior(b, f"S{u}", i) + 1)
                else:
                    nc.vector.wait_ge(y.exp, UNITS * i + u + 1)
                dve.after(nc.vector.reciprocal(exp_rec[0:n, u:u + 1], exp_sum[0:n, u:u + 1]))
                w = T if mla else na_width(x)
                nc.vector.tensor_scalar(prob[0:n, u % 5, 0:w], prob[0:n, u % 5, 0:w], exp_rec[0:n, u:u + 1], None,
                                        ALU.mult).then_inc(y.prob, 1)

            def lo_of_transposed(name, i, step):
                u = int(name[1])
                x = u % 5
                (q0, n), p = block_at(x), 2 + u % 2
                nc.vector.wait_ge(y.p_hi, UNITS * step + u + 1)
                a, z = (0, 4) if mla else NA_KEYS[x]
                if z > a:
                    nc.vector.tensor_tensor(p_lo[:, 1 + a:1 + z, q0:q0 + n], blocks(p, z - a, n),
                                            p_hi[:, 1 + a:1 + z, q0:q0 + n], ALU.subtract)
                nc.vector.tensor_tensor(p_lo[0:META, 0, q0:q0 + n], ps[0:META, 2 * p + 1, 0:n],
                                        p_hi[0:META, 0, q0:q0 + n], ALU.subtract).then_inc(free[p], 1)

            def step(i):
                split(0, i)
                for u in range(UNITS):
                    if u == 0:
                        if not at_start(i):
                            normalise(9, i - 1)
                        nc.vector.tensor_copy(q_scale2[:], q_scale[:, :, ds(2 * i, 2)]).then_inc(y.scale, 1)
                        nc.vector.wait_ge(y.scale, i + 1)
                    if mla and u == 2:
                        split(1, i)
                    top(u, i)
                    if u == 3:
                        nc.vector.wait_ge(y.q_hi, splits_per_step(mla) * (i + 1))
                        nc.vector.tensor_tensor(v_lo[:], val[:, :, ds(P * i, P)], v_hi[:],
                                                ALU.subtract).then_inc(y.q_lo, 1)
                    if u > 0:
                        normalise(u - 1, i)
                    if u >= 2:
                        lo_of_transposed(f"T{u - 2}", i, i)
                    elif not at_start(i):
                        lo_of_transposed(f"T{u + 8}p", i, i - 1)

            per = 2 * UNITS if mla else UNITS
            dve.enter(UNITS + UNITS * mla - 1, 0)
            step(0)
            dve.leave(1)
            with nc.vector.Fori(1, PAIRS) as i:
                dve.enter(per, i - 1)
                step(i)
            dve.leave(PAIRS - 1)
            normalise(9, PAIRS - 1)
            lo_of_transposed("T8p", PAIRS, PAIRS - 1)
            lo_of_transposed("T9p", PAIRS, PAIRS - 1)

        def pool_na_bias(j, b):
            def head(e, i):
                for r in range(ROWS):
                    if not (at_start(i) and e == 0):
                        if r == 0:
                            nc.gpsimd.wait_ge(bias_ready, 3 * (2 * i + e))
                    src = bias[ds(2 * i + e), :, :, (ROWS - 1 - r) * BLK:(2 * ROWS - 1 - r) * BLK]
                    nc.gpsimd.dma_start(raw_bias[BLK * r:BLK * (r + 1), :].rearrange("p (a k) -> p a k", a=3),
                                        src.rearrange("h c a k -> (h c) a k")).then_inc(bias_loaded, 16)
                if not at_start(i):
                    nc.gpsimd.wait_ge(na_sync.bias, UNITS * (i - 1) + 5 * e + 5)
                nc.gpsimd.wait_ge(bias_loaded, 16 * ROWS * (2 * i + e + 1))
                m0, b0 = 0, META
                for lo, hi in ((1, 3), (0, 3), (0, 2)):
                    w = P * (hi - lo)
                    nc.gpsimd.tensor_tensor(na_bias[:, e, b0:b0 + w], raw_bias[:, P * lo:P * hi],
                                            na_mask[:, m0:m0 + w], ALU.add).then_inc(bias_ready, 1)
                    m0, b0 = m0 + w, b0 + w + META

            def step(i):
                head(0, i)
                head(1, i)

            nc.gpsimd.wait_ge(pool_ready, 3)
            nc.gpsimd.wait_ge(load_c, 16 * CONSTS)
            steps(nc.gpsimd, step)

        UP = ["V0", "V1", "V2", "R"]
        UP += ["k0"] + [n for h_ in range(1, HEADS) for n in (f"k{h_}", f"s{h_ - 1}")] + [f"s{HEADS - 1}"]
        UP += ["q0"] + [n for h_ in range(1, HEADS) for n in (f"q{h_}", f"t{h_ - 1}")] + [f"t{HEADS - 1}"]

        def up_at(name):
            return UP.index(name) % 4, UP.index(name)

        def pe_up(j, b):
            def squared(name):
                p, k = up_at(name)
                nc.tensor.wait_ge(free[p], b[p] + k // 4 + 1)

            for name in UP:
                p, k = up_at(name)
                kind, n = name[0], int(name[1:] or 0)
                nc.tensor.wait_ge(free[p], b[p] + k // 4)
                if name == "V0":
                    nc.tensor.wait_ge(lat_split, QL + KL)
                    nc.tensor.wait_ge(lo_done, C_UP + 1)
                if name == "k0":
                    nc.tensor.wait_ge(lo_done, C_UP + 2)
                if kind == "q" and n % 3 == 0:
                    nc.tensor.wait_ge(lo_done, C_UP + 3 + n // 3)
                if kind == "V":
                    for a, x in enumerate(((0, 1), (2, 3), (4,))[n]):
                        q0, rows = block_at(x)
                        for t in range(KL):
                            w = weight(C_UP, t, 4 * P)
                            lt = (lat_hi[:, QL + t, q0:q0 + rows], lat_lo[:, QL + t, q0:q0 + rows])
                            for i, (l, r) in enumerate(((lt[0], w[0]), (lt[1], w[0]), (lt[0], w[1]))):
                                mm = nc.tensor.matmul(ps[0:rows, 2 * p + a, :], l, r, start=t == 0 and i == 0,
                                                      stop=t == KL - 1 and i == 2)
                elif kind == "k":
                    for t in range(KL):
                        w = [z[:, n * NOPE:(n + 1) * NOPE] for z in weight(C_UP + 1, t, 4 * P)]
                        mm = three_passes(pair(p), w, (lat_hi[:, QL + t, :], lat_lo[:, QL + t, :]), t == 0,
                                          t == KL - 1, NOPE)
                elif kind == "q":
                    for t in range(QL):
                        w = [z[:, n % 3 * QK:(n % 3 + 1) * QK] for z in weight(C_UP + 2 + n // 3, t, 3 * QK)]
                        mm = three_passes(pair(p), w, (lat_hi[:, t, :], lat_lo[:, t, :]), t == 0, t == QL - 1, QK)
                elif kind == "s":
                    squared(f"k{n}")
                    for a in range(2):
                        mm = nc.tensor.matmul(pair(p)[0:QK, a, :], ones[0:QK, 0:QK],
                                              sq[0:QK, n % 2, a * HALF:(a + 1) * HALF], start=True, stop=True)
                else:
                    if kind == "t":
                        squared(f"q{n}")
                        for x in range(5):
                            q0, rows = block_at(x)
                            nc.tensor.matmul(ps[0:rows, 2 * p, STAT + 2 * x:STAT + 2 * x + 2],
                                             sq[0:QK, n % 2, q0:q0 + rows], ones[0:QK, 0:2], start=True, stop=True)
                    src = m_q[:, n, :] if kind == "t" else rot_k
                    for a in range(2):
                        mm = nc.tensor.matmul(pair(p)[0:QK, a, :], mat[NOPE:QK, 2, 0:QK],
                                              src[NOPE:QK, a * HALF:(a + 1) * HALF], start=True, stop=True)
                mm.then_inc(jobs, 1)

        def act_up(j, b):
            for t in range(QL + KL):
                nc.scalar.activation(lat_hi[:, t, :], lat[:, t, :], ACT.Copy).then_inc(lat_hi_done, 1)
            for name in UP:
                p, k = up_at(name)
                kind, n = name[0], int(name[1:] or 0)
                if kind == "R":
                    continue
                nc.scalar.wait_ge(jobs, j + k + 1)
                if name == "V0":
                    nc.scalar.activation(val[0:META, 0, :], ps[0:META, 2 * p, :], ACT.Copy)
                    nc.scalar.activation(val[:, 1, :], ps[:, 2 * p + 1, :], ACT.Copy).then_inc(free[p], 1)
                elif name == "V1":
                    nc.scalar.activation(val[:, 2:4, :], ps[:, 2 * p:2 * p + 2, :], ACT.Copy).then_inc(free[p], 1)
                elif name == "V2":
                    nc.scalar.activation(val[:, 4, :], ps[:, 2 * p, :], ACT.Copy).then_inc(free[p], 1)
                    split_hi(C_UP + 3, 0, j + k + 1)
                    for e in range(2):
                        nc.scalar.activation(sq[NOPE:QK, e, :], rot_sq[NOPE:QK, :], ACT.Copy)
                elif kind == "k":
                    if n == 0:
                        nc.scalar.wait_ge(rot_ready, 1)
                    nc.scalar.activation(m_k[NOPE:QK, n, :], rot_k[NOPE:QK, :], ACT.Copy)
                    nc.scalar.activation(two(m_k[0:NOPE, n, :]), pair(p)[0:NOPE], ACT.Copy,
                                         scale=gain[0:NOPE, G_MK:G_MK + 1])
                    nc.scalar.activation(two(sq[0:NOPE, n % 2, :]), pair(p)[0:NOPE], ACT.Square).then_inc(free[p], 1)
                    if n == HEADS - 1:
                        split_hi(C_UP + 4, 0, j + k + 1)
                elif kind == "s":
                    nc.scalar.wait_ge(rms_read, 2 + PAIRS + n)
                    nc.scalar.activation(two(rms[0:QK, :]), pair(p)[0:QK], ACT.Sqrt, bias=eps[0:QK, 0:1],
                                         scale=1.0 / QK).then_inc(free[p], 1)
                elif kind == "q":
                    nc.scalar.activation(two(m_q[0:QK, n, :]), pair(p)[0:QK], ACT.Copy,
                                         scale=gain[0:QK, G_MQ:G_MQ + 1])
                    nc.scalar.activation(two(sq[0:QK, n % 2, :]), pair(p)[0:QK], ACT.Square).then_inc(free[p], 1)
                    if n in (2, 5, 7):
                        split_hi(C_UP + 5 + n // 3, 0, j + k + 1)
                else:
                    nc.scalar.activation(q_scale[:, 1:5, n], ps[:, 2 * p, STAT + 2:STAT + 10:2], ACT.Sqrt,
                                         bias=eps[:, 2:3])
                    nc.scalar.activation(q_scale[0:META, 0, n:n + 1], ps[0:META, 2 * p, STAT:STAT + 1], ACT.Sqrt,
                                         bias=eps[0:META, 2:3]).then_inc(m_stat_read, 1)

        def dve_up(j, b):
            def turn(dst, p, done):
                rows = slice(NOPE, QK)
                nc.vector.tensor_tensor(two(hid[rows, :]), pair(p)[rows], two(sin[rows, :]),
                                        ALU.mult).then_inc(free[p], 1)
                dve.after(nc.vector.tensor_tensor(dst, dst, cos[rows, :], ALU.mult))
                nc.vector.tensor_tensor(dst, dst, hid[rows, :], ALU.add).then_inc(done, 1)

            for t in range(QL + KL):
                nc.vector.wait_ge(lat_hi_done, t + 1)
                nc.vector.tensor_tensor(lat_lo[:, t, :], lat[:, t, :], lat_hi[:, t, :],
                                        ALU.subtract).then_inc(lat_split, 1)
            for name in UP:
                p, k = up_at(name)
                kind, n = name[0], int(name[1:] or 0)
                if name == "R":
                    nc.vector.wait_ge(jobs, j + k + 1)
                    turn(rot_k[NOPE:QK, :], p, rot_ready)
                elif name == "V2":
                    split_lo(C_UP + 3, 0)
                elif name == f"k{HEADS - 1}":
                    split_lo(C_UP + 4, 0)
                elif kind == "s":
                    nc.vector.wait_ge(free[p], b[p] + k // 4 + 1)
                    nc.vector.reciprocal(rstd[0:QK, :], rms[0:QK, :]).then_inc(rms_read, 1)
                    nc.vector.wait_ge(rms_read, 3 + PAIRS + n)
                    nc.vector.tensor_tensor(m_k[0:QK, n, :], m_k[0:QK, n, :], rstd[0:QK, :],
                                            ALU.mult).then_inc(m_done, 1)
                    nc.vector.wait_ge(m_done, n + 1)
                elif kind == "q" and n in (2, 5, 7):
                    split_lo(C_UP + 5 + n // 3, 0)
                elif kind == "t":
                    nc.vector.wait_ge(m_done, HEADS + n)
                    nc.vector.wait_ge(m_stat_read, n + 1)
                    turn(m_q[NOPE:QK, n, :], p, m_done)
            nc.vector.wait_ge(m_done, 2 * HEADS)
            dve.after(nc.vector.reciprocal(q_scale[:], q_scale[:]))

        def pe_merge(j, b):
            with nc.tensor.Fori(0, DK) as i:
                for p in range(4):
                    c = C_GATE + min(p, 2)
                    nc.tensor.wait_ge(lo_done, c + 1 + 3 * i)
                    nc.tensor.wait_ge(free[p], b[p] + i)
                    if p < 2:
                        for t in range(DK):
                            mm = three_passes(pair(p), weight(c, t), x_tile(t), t == 0, t == DK - 1)
                    else:
                        if p == 2:
                            nc.tensor.wait_ge(o_split, 8)
                        for t in range(4):
                            k = 4 * (3 - p) + t
                            mm = three_passes(pair(p), weight(c, 4 * (p - 2) + t), (o_hi[:, k, :], o_lo[:, k, :]),
                                              t == 0, t == 3)
                    mm.then_inc(jobs, 1)

        def act_merge(j, b):
            nc.scalar.wait_ge(free[1], b[1])
            for t in range(8):
                nc.scalar.activation(o_hi[:, t, :], o[:, t, :], ACT.Copy).then_inc(o_hi_done, 1)
            with nc.scalar.Fori(0, DK) as i:
                for p, gate in enumerate((gate_a, gate_b)):
                    nc.scalar.wait_ge(jobs, j + 1 + p + 4 * i)
                    nc.scalar.wait_ge(free[2 + p], b[2 + p] + i)
                    nc.scalar.activation(two(gate[:]), pair(p), ACT.Sigmoid).then_inc(free[p], 1)
                    split_hi(C_GATE + 3 + p, i, j + 1 + p + 4 * i)
                nc.scalar.wait_ge(g_ready, i + 1)
                nc.scalar.activation(g_hi[:, ds(i), :].rearrange("p a t -> p (a t)"), merged[:],
                                     ACT.Copy).then_inc(g_hi_done, 1)
                split_hi(C_GATE + 5, i, j + 4 + 4 * i)

        def dve_merge(j, b):
            for t in range(8):
                nc.vector.wait_ge(o_hi_done, t + 1)
                nc.vector.tensor_tensor(o_lo[:, t, :], o[:, t, :], o_hi[:, t, :], ALU.subtract).then_inc(o_split, 1)
            with nc.vector.Fori(0, DK) as i:
                split_lo(C_GATE + 3, i)
                split_lo(C_GATE + 4, i)
                for p, (part, gate) in enumerate(((part_a, gate_a), (part_b, gate_b))):
                    nc.vector.wait_ge(jobs, j + 3 + p + 4 * i)
                    nc.vector.wait_ge(free[p], b[p] + 1 + i)
                    nc.vector.tensor_tensor(two(part[:]), pair(2 + p), two(gate[:]), ALU.mult).then_inc(free[2 + p], 1)
                nc.vector.wait_ge(free[2], b[2] + 1 + i)
                nc.vector.wait_ge(free[3], b[3] + 1 + i)
                nc.vector.tensor_tensor(merged[:], part_a[:], part_b[:], ALU.add).then_inc(g_ready, 1)
                nc.vector.wait_ge(g_hi_done, i + 1)
                nc.vector.tensor_tensor(g_lo[:, ds(i), :].rearrange("p a t -> p (a t)"), merged[:],
                                        g_hi[:, ds(i), :].rearrange("p a t -> p (a t)"),
                                        ALU.subtract).then_inc(g_split, 1)
                split_lo(C_GATE + 5, i)

        def pe_out(j, b):
            for m in range(DK):
                c, p = C_OUT + m, m % 4
                nc.tensor.wait_ge(lo_done, c + 1)
                nc.tensor.wait_ge(free[p], b[p] + m // 4)
                for t in range(DK):
                    if m == 0:
                        nc.tensor.wait_ge(g_split, t + 1)
                    mm = three_passes(pair(p), weight(c, t), (g_hi[:, t, :], g_lo[:, t, :]), t == 0, t == DK - 1)
                mm.then_inc(jobs, 1)

        def act_out(j, b):
            for m in range(DK - 1):
                split_hi(C_OUT + 3 + m, 0, j + 1 + m)

        def dve_out(j, b):
            for m in range(DK):
                nc.vector.wait_ge(jobs, j + 1 + m)
                nc.vector.tensor_tensor(two(h[:, m, :]), pair(m % 4), two(h[:, m, :]), ALU.add).then_inc(free[m % 4], 1)
                split_lo(C_OUT + 3 + m, 0)

        def more(b, *n):
            return [x + y for x, y in zip(b, n)]

        b1, j1 = [0, 0, 1, 0], 1
        b2, j2 = after_ffn(b1, j1)
        b_lat, j_lat = more(b2, 0, 0, 1, 0), j2 + 1
        b_na, j_na = more(b_lat, 2, 2, 2, 2), j_lat + 8
        b_att, j_att = more(b_na, 4, 4, 4, 4), j_na + 16
        b_up, j_up = more(b_att, 24, 24, 20, 20), j_att + 88
        b_mla, j_mla = more(b_up, *[len(UP[p::4]) for p in range(4)]), j_up + len(UP)
        b_mrg, j_mrg = more(b_mla, 24, 24, 20, 20), j_mla + 88
        b_out, j_out = more(b_mrg, DK, DK, DK, DK), j_mrg + 4 * DK
        b3, j3 = more(b_out, 2, 2, 2, 2), j_out + DK
        b4, j4 = more(b3, 0, 0, 1, 0), j3 + 1

        block = ctx.enter_context(nc.Block())

        @block.sync
        def _(sp):
            def load_piece(c, i=0):
                s = c % SLOTS
                wait(sp, lo_done, c - 2 + 3 * i)
                sp.dma_start(w_raw[:, s, :], weights[ds(c + 3 * i)].rearrange("a p e -> (a p) e")).then_inc(loaded[s], 16)

            for m in range(DK):
                sp.dma_start(h[:, m, :], xT[m]).then_inc(load_x[m], 16)
            for c in range(SLOTS):
                load_piece(c)
            sp.dma_start(gain[:], gains).then_inc(load_c, 16)
            sp.dma_start(mat[:], mats).then_inc(load_c, 16)
            sp.dma_start(cos[NOPE:QK, :], rope[0]).then_inc(load_c, 16)
            sp.dma_start(sin[NOPE:QK, :], rope[1]).then_inc(load_c, 16)
            sp.dma_start(na_mask[:], mask).then_inc(load_c, 16)
            with sp.Fori(0, N_PIECES // SLOTS - 1) as i:
                for c in range(SLOTS, 2 * SLOTS):
                    load_piece(c, i)
            for c in range(N_PIECES // SLOTS * SLOTS, N_PIECES):
                load_piece(c)
            for m, done in enumerate(ffn_h_ready(b4)):
                sp.wait_ge(*done)
                sp.dma_start(out[m], h[:, m, META:]).then_inc(stored, 16)
            sp.wait_ge(stored, 16 * DK)

        @block.tensor
        def _(pe):
            pe.wait_ge(const_ready, 4)
            pe_norm_sums(0, 2, 0)
            pe_ffn(0, 0, C_FFN1, b1)
            pe_norm_sums(1, 2, b2[2])
            pe.wait_ge(load_c, 16 * CONSTS)
            pe_latents(j_lat, b_lat)
            pe_na_heads(j_na, b_na)
            pe_attention(False, na_sync, j_att, b_att)
            pe_up(j_up, b_up)
            pe_attention(True, m_sync, j_mla, b_mla)
            pe_merge(j_mrg, b_mrg)
            pe_out(j_out, b_out)
            pe_norm_sums(2, 2, b3[2])
            pe_ffn(1, 2, C_FFN2, b4)

        @block.scalar
        def _(act):
            act.wait_ge(const_ready, 4)
            act_norm_squares(0, 2, 1, [(load_x[m], 16) for m in range(DK)])
            for c in range(SLOTS):
                split_hi(c, 0, 0)
            act_norm_hi(0)
            act_ffn(C_FFN1, b1, j1, 0)
            split_hi(C_LAT + 1, 0, down_tile_job(j1, DK - 1, FC - 1))
            act_norm_squares(1, 2, j2 + 1, ffn_h_ready(b1))
            split_hi(C_LAT + 2, 0, down_tile_job(j1, DK - 1, FC))
            act_norm_hi(1)
            act_latents(j_lat, b_lat)
            act_na_heads(j_na, b_na)
            act_attention(False, na_sync, j_att, b_att)
            act_up(j_up, b_up)
            act_attention(True, m_sync, j_mla, b_mla)
            act_merge(j_mrg, b_mrg)
            act_out(j_out, b_out)
            act_norm_squares(2, 2, j3 + 1, [(free[m % 4], b_out[m % 4] + m // 4 + 1) for m in range(DK)])
            split_hi(C_FFN2 + 2, 0, j_out + DK)
            act_norm_hi(2)
            act_ffn(C_FFN2, b4, j4, 1)

        @block.vector
        def _(eng):
            eng.memset(ones[:], 1.0).then_inc(const_ready, 1)
            for k, factor in enumerate((1, HD, QK)):
                eng.memset(eps[:, k:k + 1], EPS * factor).then_inc(const_ready, 1)
            for c in range(SLOTS):
                split_lo(c, 0)
            eng.wait_ge(load_c, 16 * CONSTS)
            dve_norm(0, 2, 0, G_FFN1)
            dve_ffn(C_FFN1, b1, j1, 0)
            split_lo(C_LAT + 1, 0)
            split_lo(C_LAT + 2, 0)
            dve_norm(1, 2, b2[2], G_MIX)
            dve_latents(j_lat, b_lat)
            eng.wait_ge(pool_ready, 3)
            dve_na_heads(j_na, b_na)
            dve_attention(False, na_sync, j_att, b_att)
            dve_up(j_up, b_up)
            dve_attention(True, m_sync, j_mla, b_mla)
            dve_merge(j_mrg, b_mrg)
            dve_out(j_out, b_out)
            dve_norm(2, 2, b3[2], G_FFN2)
            dve_ffn(C_FFN2, b4, j4, 1)

        @block.gpsimd
        def _(pool):
            pool.memset(val[:, 0, :], 0.0).then_inc(pool_ready, 1)
            pool.memset(na_bias[:], 0.0).then_inc(pool_ready, 1)
            pool.memset(q_scale[:], 1.0).then_inc(pool_ready, 1)
            pool_ffn(0)
            pool_na_bias(j_att, b_att)
            pool_ffn(1)


def token_order():
    real = np.arange(SEQ).reshape(8, 4, 16).transpose(1, 0, 2).reshape(-1)
    return real


def column_pieces(w):
    n = w.shape[1] // P
    return w.reshape(DK, P, n, P).transpose(2, 1, 0, 3).reshape(n, P, PIECE)


def ffn_pieces(gate, up, down):
    g, u, d = column_pieces(gate), column_pieces(up), down.reshape(FC, P, D)
    order = [g[0], u[0]]
    for i in range(1, FC):
        order += [g[i], u[i], d[i - 1]]
    return order + [d[FC - 1]]


def padded(piece):
    return np.concatenate([piece, np.zeros((P, PIECE - piece.shape[1]), np.float32)], 1)[None]


def mixer_pieces(a):
    w = a["w_in"][0]
    lat, na, gates = w[:, :640], w[:, 672:2208], w[:, 2208:]
    rot = np.zeros((D, P), np.float32)
    rot[:, NOPE:QK] = w[:, 640:672]
    pieces = [column_pieces(rot), column_pieces(lat)]
    q, k, v = (column_pieces(na[:, 512 * n:512 * n + 512]) for n in range(3))
    pieces.append(np.stack([q, k, v], 1).reshape(-1, P, PIECE))
    ukv = a["mla_w_ukv"][0].reshape(KL, P, HEADS, 2, NOPE)
    for n in (1, 0):
        pieces.append(ukv[:, :, :, n].transpose(1, 0, 2, 3).reshape(1, P, PIECE))
    uq = a["mla_w_uq"][0].reshape(QL, P, HEADS * QK)
    for n in range(3):
        three = uq[:, :, 3 * QK * n:3 * QK * (n + 1)]
        full = np.zeros((QL, P, 3 * QK), np.float32)
        full[:, :, :three.shape[2]] = three
        pieces.append(padded(full.transpose(1, 0, 2).reshape(P, -1)))
    ga, gb = column_pieces(gates[:, :D]), column_pieces(gates[:, D:])
    ab = column_pieces(np.concatenate([a["w_branch_a"][0], a["w_branch_b"][0]]))
    pieces.append(np.stack([ga, gb, ab], 1).reshape(-1, P, PIECE))
    pieces.append(column_pieces(a["w_out"][0]))
    return np.concatenate(pieces)


def gain_columns(a):
    whole = [a[n][0].reshape(-1, P) for n in ("ffn1_norm", "mix_norm", "ffn2_norm", "mla_q_a_norm", "mla_kv_a_norm")]
    heads = [np.tile(a[n][0], 2)[None] for n in ("na_q_head_norm", "na_k_head_norm")]
    heads += [np.concatenate([a[n][0], np.zeros(P - QK, np.float32)])[None] for n in ("mla_q_head_norm", "mla_k_head_norm")]
    return np.ascontiguousarray(np.concatenate(whole + heads).T)


def constant_matrices():
    m = np.zeros((P, 3, P), np.float32)
    m[:, 0] = np.eye(P)
    m[:HD, 1, :HD] = m[HD:, 1, HD:] = 1
    for r in range(ROPE // 2):
        m[NOPE + ROPE // 2 + r, 2, NOPE + r] = -1
        m[NOPE + r, 2, NOPE + ROPE // 2 + r] = 1
    return m


def rotary_tables(real):
    pos = np.concatenate([np.arange(META), META + real]).astype(np.float32)
    half = ROPE // 2
    inv = np.float32(10000.0) ** (-np.arange(half, dtype=np.float32) / half)
    angle = inv[:, None] * pos[None]
    return np.stack([np.tile(f(angle), (2, 1)) for f in (np.cos, np.sin)]).astype(np.float32)


def window_mask():
    parts = []
    for x in (1, 2, 4):
        lo, hi = NA_KEYS[x]
        col = BLK * (x - 1) + np.arange(BLK)
        start = np.clip(col - BLK // 2, 0, 4 * BLK - BLK)
        key = BLK * lo + np.arange(BLK * (hi - lo))
        inside = (key[None] >= start[:, None]) & (key[None] < start[:, None] + BLK)
        m = np.where(inside, 0, NEG).reshape(1, BLK, hi - lo, 1, BLK)
        parts.append(np.broadcast_to(m, (ROWS, BLK, hi - lo, ROWS, BLK)).reshape(P, -1))
    return np.concatenate(parts, 1).astype(np.dtype("bfloat16"))


def bias_diagonals(rel):
    heads, rows, reach = rel.shape
    g = np.zeros((heads, BLK, rows, 3 * BLK), np.float32)
    for c in range(BLK):
        g[:, c, :, c + 1:c + 1 + reach] = rel
    return np.ascontiguousarray(g.reshape(heads, BLK, rows, 3, BLK).transpose(0, 1, 3, 2, 4)).reshape(
        heads, BLK, 3, rows * BLK)


def kernel(**inputs):
    import concourse.bacc as bacc
    from concourse.bass_utils import run_bass_kernel_spmd

    a = {k: np.asarray(v) for k, v in inputs.items()}
    real = token_order()
    x = np.concatenate([a["meta_tokens"], a["x"][0][real]])
    ffn1, ffn2 = (ffn_pieces(*(a[f"ffn{n}_w_{k}"][0] for k in ("gate", "up", "down"))) for n in (1, 2))
    arrays = {
        "weights": np.concatenate([np.stack(ffn1), mixer_pieces(a), np.stack(ffn2)]),
        "xT": np.ascontiguousarray(x.T.reshape(DK, P, T)),
        "gains": gain_columns(a),
        "mats": constant_matrices(),
        "rope": rotary_tables(real),
        "mask": window_mask(),
        "bias": bias_diagonals(a["na_rel_bias"][0]),
    }
    nc = bacc.Bacc("TRN2", target_bir_lowering=False, num_devices=1)
    args = [nc.dram_tensor(n, v.shape, mybir.dt.from_np(v.dtype), kind="ExternalInput").ap()
            for n, v in arrays.items()]
    outT = nc.dram_tensor("outT", (DK, P, SEQ), F32, kind="ExternalOutput").ap()
    build(nc, *args, outT)
    got = run_bass_kernel_spmd(nc, [arrays], core_ids=[0]).results[0]["outT"].reshape(D, SEQ)
    result = np.empty((SEQ, D), np.float32)
    result[real] = got.T
    return result[None]
```

```python
from contextlib import ExitStack

import numpy as np

import concourse.bass as bass
from concourse import mybir

F32 = mybir.dt.float32
F32R = mybir.dt.float32r
BF16 = mybir.dt.bfloat16
ALU = mybir.AluOpType
ACT = mybir.ActivationFunctionType
AX = mybir.AxisListType

P = 128
D = 1024
DK = D // P
SEQ = 512
META = 16
T = SEQ + META
HALF = T // 2
FF = 2816
FC = FF // P
EPS = 1e-6
CONSTS = 4
PIECE = 1024
SLOTS = 3

HEADS = 8
PAIRS = HEADS // 2
QK = 96
NOPE = 64
ROPE = 32
HD = 64
QL = 384 // P
KL = 256 // P
ROWS = 8
BLK = 16
NEG = -1e30

G_FFN1, G_MIX, G_FFN2, G_QA, G_KVA, G_NAQ, G_NAK, G_MQ, G_MK = 0, 8, 16, 24, 27, 29, 30, 31, 32

C_FFN1 = 0
C_LAT = C_FFN1 + 3 * FC
C_NA = C_LAT + 6
UP_W = KL * P + QL * 2 * P

NA_FIRST = ("g1:0:8 .g1 S0 q:0:3 S1 q:3:6 S2 .vs T0 q:6:8 .q S3 T1 k:0:3 S4 T2 k:3:8 .k S5 T3 v:0:2 S6 T4 st .st "
            "v:2:4 S7 PV0 T5 v:4:6 .na S8 T6 v:6:8 .v S9 T7 .nb vt .vt")
NA_STEP = ("T8p q:0:5 S0 T9p q:5:7 S1 PVp q:7:8 .q S2 .vs T0 k:0:3 S3 T1 k:3:6 S4 T2 k:6:8 .k S5 T3 v:0:2 S6 T4 "
           "st .st v:2:4 S7 PV0 T5 v:4:6 .na S8 T6 v:6:8 .v S9 T7 .nb vt .vt")
NA_LAST = ("T8p S0 T9p S1 .u PVp k0 .k0 S2 T0 q0 .q0 S3 .vs T1 z0 .z0 .t0 S4 T2 .a0 V0 .V0 S5 T3 .b0 V1 .V1 S6 "
           "T4 V2 .V2 S7 PV0 k1 .k1 T5 S8 q1 .q1 T6 S9 T7 z1 .z1 .t1")
M_FIRST = ("g3:0:8 .g3 S0 .u g1:0:4 S1 .e g1:4:8 .g1 S2 .f T0 g4:0:4 S3 .vs T1 g4:4:8 .g4 k0 .k0 S4 .s T2 q0 .q0 "
           "S5 T3 z0 .z0 .t0 S6 T4 k1 .k1 .a0 q1 .q1 S7 .b0 z1 PV0 .z1 .t1 T5 g0:0:3 S8 T6 .a1 g0:3:6 "
           "S9 T7 .b1 g0:6:8 .g0")
M_STEP = ("g0:0:3 T8p g0:3:8 .g0 S0 T9p g1:0:4 S1 g1:4:8 .g1 .u PVp S2 T0 k0 .k0 S3 .vs T1 q0 .q0 S4 .s T2 z0 "
          ".z0 .t0 S5 T3 k1 .k1 S6 T4 .a0 q1 .q1 S7 z1 PV0 .b0 .z1 .t1 T5 g2:0:3 S8 T6 .a1 g2:3:6 S9 T7 .b1 g2:6:8 .g2")
M_LAST = ("g1:0:3 T8p g1:3:8 .g1 S0 T9p g0:0:3 S1 g0:3:5 PVp g0:5:8 .g0 S2 T0 g2:0:4 S3 .vs T1 g2:4:8 .g2 S4 .s "
          "T2 g3:0:3 S5 T3 g3:3:5 S6 T4 g3:5:8 .g3 S7 PV0 g4:0:4 T5 g4:4:8 .g4 S8 T6 S9 T7")
DRAIN = "T8p T9p PVp"
S_PAIR, T_PAIR = 0, 2
ODD_PAIR = {n: 1 for n in ("PV0", "PVp", "k", "st", "vt", "g1", "g2", "k0", "k1", "V0", "V2")}
UNITS = 10
PROB = (0, 1, 2, 0, 1, 2, 0, 1, 2, 3)
PROB_USER = ("T6", "T7", "T8p", "T0", "T1", "T2", "T3", "T4", "T5", "T9p")
PARTS = {n: DK for n in ("v", "q", "k", "g0", "g1", "g2", "g3", "g4")}
STREAM = [n for order in (NA_FIRST, NA_STEP, NA_STEP, NA_LAST, M_FIRST, M_STEP, M_STEP, M_LAST)
          for n in (x.split(":")[0] for x in order.split() if x == "V0" or x.split(":")[1:2] == ["0"])]
C_STEPS = C_NA + 3
C_V = C_STEPS + STREAM.index("V0")
C_BRANCH = C_STEPS + len(STREAM)
C_OUT = C_BRANCH + DK
C_FFN2 = C_OUT + DK
N_PIECES = C_FFN2 + 3 * FC
NA_KEYS = ((0, 0), (0, 2), (0, 3), (1, 4), (2, 4))


def psum_pair(name):
    return S_PAIR if name[0] == "S" else T_PAIR if name[0] == "T" else ODD_PAIR.get(name, 3)


class Plan:

    def __init__(self, j, b, c, g, first, step, last):
        self.j, self.b, self.c, self.g = j, b, c, g
        work = [[(n, int(lo or 0), int(hi or 1)) for n, lo, hi in ((x + "::").split(":")[:3] for x in o.split())]
                for o in (first, step, last, DRAIN)]
        self.work = [work[0], work[1], work[1], work[2], work[3]]
        self.jobs = [[n for n, lo, hi in w if hi == PARTS.get(n, 1) or (lo, hi) == (0, 1) and n not in PARTS]
                     for w in self.work]
        self.jobs = [[n for n in names if n[0] != "."] for names in self.jobs]
        self.pieces = [[n for n in names if n in PARTS or n == "V0"] for names in self.jobs]

    def _count(self, start, i, names, name):
        here = [n for n in self.jobs[i if isinstance(i, int) else 1] if n in names]
        at = here.index(name) if name in here else len([n for n in here if n in names])
        if isinstance(i, int):
            return start + sum(n in names for step in self.jobs[:i] for n in step) + at
        per = sum(n in names for n in self.jobs[1])
        return start + sum(n in names for n in self.jobs[0]) - per + at + per * i

    def job(self, name, i):
        return self._count(self.j, i, {n for w in self.jobs for n in w}, name) + 1

    def job_before(self, name, i):
        tails = [w[w.index(name):] for w in self.jobs[:2]]
        assert isinstance(i, int) or len(tails[0]) == len(tails[1])
        return self.job(name, i - 1)

    def prior(self, name, i):
        p = psum_pair(name)
        return self._count(self.b[p], i, {n for w in self.jobs for n in w if psum_pair(n) == p}, name)

    def _place(self, start, i, steps, name):
        if isinstance(i, int):
            return start + sum(map(len, steps[:i])) + steps[i].index(name), 0
        return start + len(steps[0]) - len(steps[1]) + steps[1].index(name), len(steps[1])

    def piece(self, name, i):
        c, per = self._place(self.c, i, self.pieces, name)
        assert per % SLOTS == 0
        return c, per // SLOTS * i if per else 0

    def gate(self, name, i):
        g, per = self._place(self.g, i, [[n for n in w if n[0] == "g"] for w in self.pieces], name)
        return g + per * i if per else g

    def at(self, name, i):
        return psum_pair(name), self.job(name, i), self.prior(name, i)

    def after(self):
        every = [n for w in self.jobs for n in w]
        return ([self.b[p] + sum(psum_pair(n) == p for n in every) for p in range(4)], self.j + len(every),
                self.c + sum(map(len, self.pieces)), self.g + sum(n[0] == "g" for n in every))


def ds(start, n=1):
    return slice(start, start + n) if isinstance(start, int) else bass.ds(start, n)


def at_start(i):
    return isinstance(i, int) and i == 0


def block_at(x):
    return (0, META) if x == 0 else (META + P * (x - 1), P)


class Own:

    def __init__(self, eng, semaphore):
        self.eng, self.semaphore = eng, semaphore
        self.base = self.n = self.per = self.i = 0

    def after(self, instruction):
        instruction.then_inc(self.semaphore, 1)
        self.n += 1
        self.eng.wait_ge(self.semaphore, self.base + self.n + (self.per * self.i if self.per else 0))

    def enter(self, per, i):
        self.base, self.n, self.per, self.i = self.base + self.n, 0, per, i

    def leave(self, steps):
        assert self.n == self.per, (self.n, self.per)
        self.base, self.n, self.per = self.base + self.per * steps, 0, 0


def build(nc, weights, up_weights, xT, gains, mats, rope, mask, bias, gates, out):
    n_pieces = weights.shape[0]
    assert n_pieces == N_PIECES
    with ExitStack() as ctx:
        def sb(name, shape, dt=F32):
            return ctx.enter_context(nc.sbuf_tensor(name, shape, dt))

        def sem(name):
            return ctx.enter_context(nc.semaphore(name))

        TILE = 4 * T
        place = [nc.sbuf_base + -nc.sbuf_base % 32]

        def take(size):
            place[0] += size
            return place[0] - size

        def at(name, byte, shape, dt=F32):
            return nc.alloc_sbuf_tensor_at(name, shape, dt, offset=byte)

        h = at("h", take(8 * TILE), [P, DK, T])
        x_hi = at("x_hi", take(8 * TILE), [P, DK, T], F32R)
        x_lo = at("x_lo", take(8 * TILE), [P, DK, T], F32R)
        w_raw = at("w_raw", take(4 * SLOTS * PIECE), [P, SLOTS, PIECE])
        w_hi = at("w_hi", take(4 * SLOTS * PIECE), [P, SLOTS, PIECE], F32R)
        w_lo = at("w_lo", take(4 * SLOTS * PIECE), [P, SLOTS, PIECE], F32R)
        gain = at("gain", take(160), [P, gains.shape[1]])
        mat = at("mat", take(8 * P), [P, 2, P])
        ones = at("ones", take(4 * P), [P, P])
        table = at("table", take(32), [P, 1])
        eps = at("eps", take(32), [P, 3])
        q_rms = at("q_rms", take(64), [P, 5, 2])
        q_scale = at("q_scale", take(64), [P, 5, 2])
        neg_max = at("neg_max", take(64), [P, UNITS])
        exp_bias = at("exp_bias", take(64), [P, UNITS])
        exp_sum = at("exp_sum", take(64), [P, UNITS])
        exp_rec = at("exp_rec", take(64), [P, UNITS])

        hid_at = take(2 * TILE)
        hid_hi = at("hid_hi", hid_at, [P, T], F32R)
        hid_lo = at("hid_lo", hid_at + TILE, [P, T], F32R)
        rot_k = at("rot_k", hid_at, [P, T])
        rot_sq = at("rot_sq", hid_at + TILE, [P, T])
        pm_hi = at("pm_hi", hid_at, [META, T], F32R)
        pm_lo = at("pm_lo", hid_at + TILE, [META, T], F32R)

        scratch = take(6 * TILE)
        silu = at("silu", scratch, [P, T])
        hid = at("hid", scratch + TILE, [P, T])
        xs = at("xs", scratch + 2 * TILE, [P, 2, T])
        sq = at("sq", scratch + 4 * TILE, [P, 2, T])
        prob = at("prob", scratch, [P, 4, T])
        gated = [at(f"gated{k}", scratch + n * TILE, [P, 2, T])
                 for k, n in enumerate((4, 0, 2))]
        rms = at("rms", take(TILE), [P, T])
        rstd = at("rstd", take(TILE), [P, T])

        MASK_W = sum(P * (b - a) for a, b in (NA_KEYS[1], NA_KEYS[2], NA_KEYS[4]))
        late = take(2 * TILE + 2 * MASK_W + 8 * (MASK_W + 3 * META))
        cos = at("cos", late, [P, T])
        sin = at("sin", late + TILE, [P, T])
        na_mask = at("na_mask", late + 2 * TILE, [P, MASK_W], BF16)
        na_bias = at("na_bias", late + 2 * TILE + 2 * MASK_W, [P, 2, MASK_W + 3 * META])

        m_s = [at(f"m_{n}", late + (2 + k) * TILE, [P, T], F32R)
               for k, n in enumerate(("q_hi", "q_lo", "k_hi", "k_lo"))]
        assert late + 6 * TILE <= place[0]

        mix = place[0]
        lat_hi = at("lat_hi", take(5 * TILE), [P, QL + KL, T], F32R)
        lat_lo = at("lat_lo", take(5 * TILE), [P, QL + KL, T], F32R)
        val = at("val", take(80 * P), [P, 5, 4 * P])
        pt_at = take(8 * TILE)
        p_hi = at("p_hi", pt_at, [P, 4, T], F32R)
        p_lo = at("p_lo", pt_at + 4 * TILE, [P, 4, T], F32R)
        v_hi = at("v_hi", take(20 * P), [P, 5, P], F32R)
        v_lo = at("v_lo", take(20 * P), [P, 5, P], F32R)
        o_at = take(8 * TILE)
        o = at("o", o_at, [P, 8, T])
        na_s = [at(f"na_{n}", o_at + (4 + k) * TILE, [P, T], F32R)
                for k, n in enumerate(("q_hi", "q_lo", "k_hi", "k_lo"))]
        gate_m = at("gate_m", o_at + 7 * TILE, [P, T])
        raw_bias = at("raw_bias", take(12 * P), [P, 3 * P])
        next_at = take(4 * TILE)
        m_q = at("m_q", next_at, [P, 2, T])
        m_k = at("m_k", next_at + 2 * TILE, [P, 2, T])
        na_v = at("na_v", next_at, [P, T])
        na_q = at("na_q", next_at + TILE, [P, T])
        na_k = at("na_k", next_at + 3 * TILE, [P, T])
        up_hi = at("up_hi", take(4 * UP_W), [P, UP_W], F32R)
        up_lo_at = take(4 * UP_W)
        gate_na = at("gate_na", up_lo_at - 4 * UP_W, [P, T])
        up_raw = at("up_raw", up_lo_at, [P, UP_W])
        up_lo = at("up_lo", up_lo_at, [P, UP_W], F32R)
        assert place[0] <= nc.sbuf_usable_end
        lat = at("lat", pt_at, [P, QL + KL, T])
        lat_sq = at("lat_sq", o_at, [P, QL + KL, T])
        o_hi = at("o_hi", mix, [P, 8, T], F32R)
        o_lo = at("o_lo", mix + 8 * TILE, [P, 8, T], F32R)
        g_hi = at("g_hi", mix + 16 * TILE, [P, DK, T], F32R)
        g_lo = at("g_lo", mix + 24 * TILE, [P, DK, T], F32R)

        ps = ctx.enter_context(nc.psum_tensor("ps", [P, 8, 512], F32))

        load_x = [sem(f"load_x{m}") for m in range(DK)]
        load_gain = sem("load_gain")
        load_c = sem("load_c")
        loaded = [sem(f"w_loaded{s}") for s in range(SLOTS)]
        hi_done = sem("w_hi_done")
        lo_done = sem("w_lo_done")
        jobs = sem("pe_jobs")
        free = [sem(f"psum_free{p}") for p in range(4)]
        const_ready = sem("const_ready")
        stored = sem("stored")
        sq_ready = sem("sq_ready")
        sq_used = sem("sq_used")
        rstd_ready = sem("rstd_ready")
        xs_ready = sem("xs_ready")
        x_hi_done = sem("x_hi_done")
        x_split = sem("x_split")
        hid_hi_done = sem("hid_hi_done")
        pool_ready = sem("pool_ready")
        small_turn = sem("small_turn")
        dve_own = sem("dve_own")
        up_loaded = sem("up_loaded")
        up_hi_done = sem("up_hi_done")
        up_split = sem("up_split")
        lat_normed = sem("lat_normed")
        lat_hi_done = sem("lat_hi_done")
        rms_read = sem("rms_read")
        na_k_ready = sem("na_k_ready")
        rot_ready = sem("rot_ready")
        m_key_normed = sem("m_key_normed")
        m_done = sem("m_query_turned")
        o_hi_done = sem("o_hi_done")
        o_split = sem("o_split")
        g_ready = sem("g_ready")
        g_hi_done = sem("g_hi_done")
        g_split = sem("g_split")
        gate_stored = sem("gate_stored")
        gate_loaded = [sem(f"gate_loaded{k}") for k in range(3)]
        gate_ready = sem("gate_ready")
        bias_loaded = sem("bias_loaded")
        bias_ready = sem("bias_ready")
        hid_split = sem("hid_split")

        def pair(p):
            return ps[:, 2 * p:2 * p + 2, 0:HALF]

        def two(ap):
            return ap.rearrange("p (a c) -> p a c", a=2)

        dve = Own(nc.vector, dve_own)

        def wait(eng, semaphore, value):
            if not isinstance(value, int) or value > 0:
                eng.wait_ge(semaphore, value)

        def split_hi(c, i, left):
            s = c % SLOTS
            nc.scalar.wait_ge(loaded[s], 16 * (c // SLOTS + 1 + i))
            wait(nc.scalar, jobs, left)
            nc.scalar.activation(w_hi[:, s, :], w_raw[:, s, :], ACT.Copy).then_inc(hi_done, 1)

        def split_lo(c, i):
            s = c % SLOTS
            nc.vector.wait_ge(hi_done, c + 1 + 3 * i)
            nc.vector.tensor_tensor(w_lo[:, s, :], w_raw[:, s, :], w_hi[:, s, :],
                                    ALU.subtract).then_inc(lo_done, 1)

        def weight(c, k, width=P):
            s = c % SLOTS
            return w_hi[:, s, k * width:(k + 1) * width], w_lo[:, s, k * width:(k + 1) * width]

        def three_passes(dst, w, r, first, last, rows=P):
            for n, (x, y) in enumerate(((w[0], r[0]), (w[0], r[1]), (w[1], r[0]))):
                for a in range(2):
                    mm = nc.tensor.matmul(dst[0:rows, a, :], x, y[:, a * HALF:(a + 1) * HALF],
                                          start=first and n == 0, stop=last and n == 2)
            return mm

        def x_tile(k):
            return x_hi[:, k, :], x_lo[:, k, :]

        def load_sqrt():
            nc.scalar.activation(table[:], eps[:, 0:1], ACT.Sqrt)

        def act_norm_squares(v, p, job, h_ready):
            for m in range(DK):
                nc.scalar.wait_ge(*h_ready[m])
                if m >= 2:
                    nc.scalar.wait_ge(sq_used, (DK - 1) * v + m - 1)
                nc.scalar.activation(sq[:, m % 2, :], h[:, m, :], ACT.Square).then_inc(sq_ready, 1)
            load_sqrt()
            nc.scalar.wait_ge(jobs, job)
            wait(nc.scalar, rstd_ready, v)
            nc.scalar.activation(two(rms[:]), pair(p), ACT.Sqrt, bias=eps[:, 0:1],
                                 scale=1.0 / D).then_inc(free[p], 1)

        def pe_norm_sums(v, p, prior):
            wait(nc.tensor, free[p], prior)
            for m in range(DK):
                nc.tensor.wait_ge(sq_ready, DK * v + m + 1)
                for a in range(2):
                    mm = nc.tensor.matmul(pair(p)[:, a, :], ones[:], sq[:, m % 2, a * HALF:(a + 1) * HALF],
                                          start=m == 0, stop=m == DK - 1)
                mm.then_inc(jobs if m == DK - 1 else sq_used, 1)

        def act_norm_hi(v):
            for m in range(DK):
                nc.scalar.wait_ge(xs_ready, DK * v + m + 1)
                nc.scalar.activation(x_hi[:, m, :], xs[:, m % 2, :], ACT.Copy).then_inc(x_hi_done, 1)

        def dve_norm(v, p, prior, g0, split_first=()):
            nc.vector.wait_ge(free[p], prior + 1)
            nc.vector.reciprocal(rstd[:], rms[:]).then_inc(rstd_ready, 1)
            for c in split_first:
                split_lo(c, 0)
            nc.vector.wait_ge(rstd_ready, v + 1)
            for m in range(DK + 1):
                if m < DK:
                    wait(nc.vector, x_split, DK * v + m - 1)
                    nc.vector.scalar_tensor_tensor(xs[:, m % 2, :], h[:, m, :], gain[:, g0 + m:g0 + m + 1],
                                                   rstd[:], ALU.mult, ALU.mult).then_inc(xs_ready, 1)
                if m > 0:
                    nc.vector.wait_ge(x_hi_done, DK * v + m)
                    nc.vector.tensor_tensor(x_lo[:, m - 1, :], xs[:, (m - 1) % 2, :], x_hi[:, m - 1, :],
                                            ALU.subtract).then_inc(x_split, 1)

        DOWN_PAIR = (2, 3, 0, 1, 2, 3, 1, 2)
        A_STEP = (2, 3, 3, 2)

        def up_prior(b, p, i):
            return b[p] if isinstance(i, int) and i == 0 else b[p] + 1 + A_STEP[p] * (i - 1)

        def down_prior(b, m, i):
            p = DOWN_PAIR[m]
            ups = 0 if p > 1 else 1 if isinstance(i, int) and i == FC else 2
            return b[p] + A_STEP[p] * (i - 1) + ups + DOWN_PAIR[:m].count(p)

        def up_job(j, which, i):
            return j + 1 + which if isinstance(i, int) and i == 0 else j + 10 * i - 7 + which

        def down_tile_job(j, m, i):
            return j + 10 * i - (7 if isinstance(i, int) and i == FC else 5) + m

        def after_ffn(b, j):
            return [b[p] + A_STEP[p] * FC for p in range(4)], j + 10 * FC

        def two_with_norm(c, split, b):
            for p in range(2):
                nc.tensor.wait_ge(lo_done, c + p + 1)
                wait(nc.tensor, free[p], b[p])
            for k in range(DK):
                nc.tensor.wait_ge(x_split, split + k + 1)
                for p in range(2):
                    mm = three_passes(pair(p), weight(c + p, k), x_tile(k), k == 0, k == DK - 1)
                    if k == DK - 1:
                        mm.then_inc(jobs, 1)

        def pe_ffn(f, v, c, b):
            def up(p, cc, ii, i):
                nc.tensor.wait_ge(lo_done, cc + 1 + 3 * ii)
                wait(nc.tensor, free[p], up_prior(b, p, i))
                for k in range(DK):
                    mm = three_passes(pair(p), weight(cc, k), x_tile(k), k == 0, k == DK - 1)
                mm.then_inc(jobs, 1)

            def down(cc, ii, i):
                nc.tensor.wait_ge(lo_done, cc + 1 + 3 * ii)
                nc.tensor.wait_ge(hid_split, FC * f + i)
                for m in range(DK):
                    p = DOWN_PAIR[m]
                    wait(nc.tensor, free[p], down_prior(b, m, i))
                    three_passes(pair(p), weight(cc, m), (hid_hi[:], hid_lo[:]), True, True).then_inc(jobs, 1)

            def step(i):
                up(0, c - 1, i, i)
                up(1, c, i, i)
                down(c + 1, i, i)

            two_with_norm(c, DK * v, b)
            step(1)
            with nc.tensor.Fori(2, FC) as i:
                step(i)
            down(c + 3 * FC - 1, 0, FC)

        def act_ffn(c, b, j, f):
            def gate(i):
                nc.scalar.wait_ge(jobs, up_job(j, 0, i))
                if not (isinstance(i, int) and i == 0):
                    nc.scalar.wait_ge(free[1], up_prior(b, 1, i - 1) + 1)
                nc.scalar.activation(two(silu[:]), pair(0), ACT.Silu).then_inc(free[0], 1)

            def hidden(i):
                nc.scalar.wait_ge(free[1], up_prior(b, 1, i) + 1)
                if not (isinstance(i, int) and i == 0):
                    nc.scalar.wait_ge(jobs, down_tile_job(j, DK - 1, i))
                nc.scalar.activation(hid_hi[:], hid[:], ACT.Copy).then_inc(hid_hi_done, 1)

            def step(i):
                split_hi(c + 1, i, down_tile_job(j, DK - 1, i - 1) if not (isinstance(i, int) and i == 1)
                         else up_job(j, 1, 0))
                gate(i)
                split_hi(c + 2, i, up_job(j, 0, i))
                if not (isinstance(i, int) and i == FC - 1 and c + 3 * FC >= n_pieces):
                    split_hi(c + 3, i, up_job(j, 1, i))
                hidden(i)

            gate(0)
            split_hi(c + 3, 0, up_job(j, 0, 0))
            hidden(0)
            step(1)
            with nc.scalar.Fori(2, FC - 1) as i:
                step(i)
            step(FC - 1)

        def dve_ffn(c, b, j, f):
            def up(i):
                nc.vector.wait_ge(jobs, up_job(j, 1, i))
                nc.vector.wait_ge(free[0], up_prior(b, 0, i) + 1)
                wait(nc.vector, hid_split, FC * f + i)
                nc.vector.tensor_tensor(two(hid[:]), pair(1), two(silu[:]), ALU.mult).then_inc(free[1], 1)

            def down(i):
                for m in range(DK):
                    nc.vector.wait_ge(jobs, down_tile_job(j, m, i))
                    nc.vector.scalar_tensor_tensor(two(h[:, m, :]), pair(DOWN_PAIR[m]), 0.5, two(h[:, m, :]),
                                                   ALU.mult, ALU.add).then_inc(free[DOWN_PAIR[m]], 1)

            def step(i):
                split_lo(c + 1, i)
                split_lo(c + 2, i)
                up(i)
                down(i)
                if not (isinstance(i, int) and i == FC - 1 and c + 3 * FC >= n_pieces):
                    split_lo(c + 3, i)

            up(0)
            split_lo(c + 3, 0)
            step(1)
            with nc.vector.Fori(2, FC - 1) as i:
                step(i)
            step(FC - 1)
            down(FC)

        def pool_ffn(f):
            with nc.gpsimd.Fori(0, FC) as i:
                nc.gpsimd.wait_ge(hid_hi_done, FC * f + 1 + i)
                nc.gpsimd.tensor_tensor(hid_lo[:], hid[:], hid_hi[:], ALU.subtract).then_inc(hid_split, 1)

        def ffn_h_ready(b):
            return [(free[DOWN_PAIR[m]], down_prior(b, m, FC) + 1) for m in range(DK)]

        def pe_latents(j, b):
            two_with_norm(C_LAT, DK, b)
            for k in range(2, 6):
                c, p = C_LAT + k, k % 4
                nc.tensor.wait_ge(lo_done, c + 1)
                wait(nc.tensor, free[p], b[p] + k // 4)
                for t in range(DK):
                    mm = three_passes(pair(p), weight(c, t), x_tile(t), t == 0, t == DK - 1)
                mm.then_inc(jobs, 1)
            for p, tiles, (last, prior) in ((2, range(QL), (3, b[3] + 1)), (3, range(QL, QL + KL), (1, b[1] + 2))):
                nc.tensor.wait_ge(free[last], prior)
                nc.tensor.wait_ge(free[p], b[p] + 1)
                for t in tiles:
                    for a in range(2):
                        mm = nc.tensor.matmul(pair(p)[:, a, :], ones[:], lat_sq[:, t, a * HALF:(a + 1) * HALF],
                                              start=t == tiles[0], stop=t == tiles[-1])
                mm.then_inc(jobs, 1)

        def act_latents(j, b):
            for k in range(6):
                p = k % 4
                nc.scalar.wait_ge(jobs, j + 1 + k)
                if k == 0:
                    nc.scalar.activation(two(rot_k[NOPE:P, :]), pair(p)[NOPE:P], ACT.Copy,
                                         scale=gain[NOPE:P, G_MK:G_MK + 1])
                    nc.scalar.activation(two(rot_sq[NOPE:QK, :]), pair(p)[NOPE:QK], ACT.Square).then_inc(free[p], 1)
                else:
                    nc.scalar.activation(two(lat[:, k - 1, :]), pair(p), ACT.Copy)
                    nc.scalar.activation(two(lat_sq[:, k - 1, :]), pair(p), ACT.Square).then_inc(free[p], 1)
                split_hi(C_LAT + 3 + k, 0, j + 1 + k)
            load_sqrt()
            for k, (p, width) in enumerate(((2, QL * P), (3, KL * P))):
                nc.scalar.wait_ge(jobs, j + 7 + k)
                if k:
                    nc.scalar.wait_ge(rms_read, 1)
                else:
                    nc.scalar.wait_ge(rstd_ready, 2)
                nc.scalar.activation(two(rms[:]), pair(p), ACT.Sqrt, bias=eps[:, 0:1],
                                     scale=1.0 / width).then_inc(free[p], 1)

        def dve_latents(j, b):
            for k in range(6):
                split_lo(C_LAT + 3 + k, 0)
            for k, (p, g, tiles) in enumerate(((2, G_QA, range(QL)), (3, G_KVA, range(QL, QL + KL)))):
                nc.vector.wait_ge(free[p], b[p] + 2)
                nc.vector.reciprocal(rstd[:], rms[:]).then_inc(rms_read, 1)
                nc.vector.wait_ge(rms_read, k + 1)
                for t in tiles:
                    col = g + t - tiles[0]
                    nc.vector.scalar_tensor_tensor(lat[:, t, :], lat[:, t, :], gain[:, col:col + 1], rstd[:],
                                                   ALU.mult, ALU.mult).then_inc(lat_normed, 1)
                nc.vector.wait_ge(lat_normed, tiles[-1] + 1)

        STAT = 272

        def token_values(dst, n, q0, w, lt, first, last):
            for k, (l, m) in enumerate(((lt[0], w[0]), (lt[1], w[0]), (lt[0], w[1]))):
                mm = nc.tensor.matmul(dst, l[:, q0:q0 + n], m, start=first and k == 0, stop=last and k == 2)
            return mm

        def pe_na_part(name, lo, hi, at, c, i):
            p, _, prior = at
            if lo == 0:
                nc.tensor.wait_ge(free[p], prior)
                if name in PARTS:
                    nc.tensor.wait_ge(lo_done, c + 1 + 3 * i)
                elif name == "vt":
                    nc.tensor.sem_inc(small_turn, 1)
            if name == "vt":
                for x in range(5):
                    q0, rows = block_at(x)
                    mm = nc.tensor.transpose(ps[0:rows, 2 * p + (x == 0), P * max(x - 1, 0):P * max(x, 1)],
                                             na_v[:, q0:q0 + rows], mat[:, 0, :])
                mm.then_inc(jobs, 1)
                return
            if name == "st":
                for x in range(5):
                    q0, n = block_at(x)
                    nc.tensor.matmul(ps[0:n, 2 * p, STAT + 2 * x:STAT + 2 * x + 2], sq[:, 1, q0:q0 + n],
                                     mat[:, 1, 0:P:HD], start=True, stop=True)
                for a in range(2):
                    mm = nc.tensor.matmul(pair(p)[:, a, :], mat[:, 1, :], sq[:, 0, a * HALF:(a + 1) * HALF],
                                          start=True, stop=True)
                mm.then_inc(jobs, 1)
                return
            for t in range(lo, hi):
                mm = three_passes(pair(p), weight(c, t), x_tile(t), t == 0, t == DK - 1)
            if hi == PARTS[name]:
                mm.then_inc(jobs, 1)

        def act_na_part(name, at, c, i, n, buffers_read):
            p, job, _ = at
            nc.scalar.wait_ge(jobs, job)
            if name == "vt":
                nc.scalar.activation(val[:, 1:5, ds(P * n, P)], ps[:, 2 * p, :].rearrange("p (x f) -> p x f", f=P),
                                     ACT.Copy)
                nc.scalar.activation(val[0:META, 0, ds(P * n, P)], ps[0:META, 2 * p + 1, 0:P],
                                     ACT.Copy).then_inc(free[p], 1)
                return
            if name == "v":
                nc.scalar.activation(two(na_v[:]), pair(p), ACT.Copy).then_inc(free[p], 1)
            elif name == "st":
                nc.scalar.activation(q_rms[:, 1:5, :],
                                     ps[:, 2 * p, STAT + 2:STAT + 10].rearrange("p (x e) -> p x e", e=2),
                                     ACT.Sqrt, bias=eps[:, 1:2])
                nc.scalar.activation(q_rms[0:META, 0, :], ps[0:META, 2 * p, STAT:STAT + 2],
                                     ACT.Sqrt, bias=eps[0:META, 1:2])
                nc.scalar.wait_ge(rms_read, 2 + 2 * n)
                nc.scalar.activation(two(rms[:]), pair(p), ACT.Sqrt, bias=eps[:, 0:1],
                                     scale=1.0 / HD).then_inc(free[p], 1)
                return
            else:
                if name == "q" and buffers_read is not None:
                    nc.scalar.wait_ge(*buffers_read)
                dst, g, k = (na_q, G_NAQ, 1) if name == "q" else (na_k, G_NAK, 0)
                nc.scalar.activation(two(dst[:]), pair(p), ACT.Copy, scale=gain[:, g:g + 1])
                nc.scalar.activation(two(sq[:, k, :]), pair(p), ACT.Square).then_inc(free[p], 1)
            split_hi(c + 3, i, job)

        def ahead(piece):
            return piece[0] + SLOTS, piece[1]

        def half_reciprocal(rows, second, count):
            cols = slice(HALF * second, HALF * (second + 1))
            nc.vector.reciprocal(rstd[rows, cols], rms[rows, cols]).then_inc(rms_read, 1)
            if second:
                nc.vector.wait_ge(rms_read, count)

        def dve_na_key(at, n, second):
            if not second:
                nc.vector.wait_ge(free[at[0]], at[2] + 1)
            half_reciprocal(slice(0, P), second, 2 + 2 * (n + 1))
            if second:
                nc.vector.tensor_tensor(na_k[:], na_k[:], rstd[:], ALU.mult).then_inc(na_k_ready, 1)
                nc.vector.wait_ge(na_k_ready, n + 1)

        def dve_m_key(at, n, e, second, shared):
            if not second:
                nc.vector.wait_ge(free[at[0]], at[2] + 1)
            half_reciprocal(slice(0, QK), second, 2 + 2 * PAIRS + 2 * (2 * n + e + 1))
            if second and not shared:
                nc.vector.tensor_tensor(m_k[0:QK, e, :], m_k[0:QK, e, :], rstd[0:QK, :],
                                        ALU.mult).then_inc(m_key_normed, 1)
                nc.vector.wait_ge(m_key_normed, 2 * n + e + 1)

        def act_gate(name, plan, i, buffer):
            (p, job, _), (c, k), g = plan.at(name, i), plan.piece(name, i), plan.gate(name, i)
            nc.scalar.wait_ge(jobs, job)
            wait(nc.scalar, gate_stored, 16 * g)
            nc.scalar.activation(two(buffer[:]), pair(p), ACT.Copy).then_inc(free[p], 1)
            split_hi(c + 3, k, job)
            nc.scalar.wait_ge(free[p], plan.prior(name, i) + 1)
            nc.scalar.dma_start(gates[ds(g)].rearrange("a p t -> (a p) t"), buffer[:]).then_inc(gate_stored, 16)

        def pe_m_part(name, at, n):
            p, _, prior = at
            kind, e = name[0], int(name[1])
            nc.tensor.wait_ge(free[p], prior)
            if name == "V0":
                nc.tensor.wait_ge(lo_done, C_V + 1)
            if kind == "V":
                for a, x in enumerate(((0, 1), (2, 3), (4,))[e]):
                    q0, rows = block_at(x)
                    for t in range(KL):
                        mm = token_values(ps[0:rows, 2 * p + a, :], rows, q0, weight(C_V, t, 4 * P),
                                          (lat_hi[:, QL + t, :], lat_lo[:, QL + t, :]), t == 0, t == KL - 1)
            elif kind == "k":
                if e == 0:
                    nc.tensor.wait_ge(up_split, n + 1)
                for t in range(KL):
                    w = [z[:, P * t + NOPE * e:P * t + NOPE * (e + 1)] for z in (up_hi, up_lo)]
                    mm = three_passes(pair(p), w, (lat_hi[:, QL + t, :], lat_lo[:, QL + t, :]), t == 0,
                                      t == KL - 1, NOPE)
            elif kind == "q":
                for t in range(QL):
                    first = KL * P + 2 * P * t + P * e
                    w = [z[:, first:first + P] for z in (up_hi, up_lo)]
                    mm = three_passes(pair(p), w, (lat_hi[:, t, :], lat_lo[:, t, :]), t == 0, t == QL - 1)
            elif kind == "z":
                for x in range(5):
                    q0, rows = block_at(x)
                    nc.tensor.matmul(ps[0:rows, 2 * p, STAT + 2 * x:STAT + 2 * x + 2], sq[0:QK, 1, q0:q0 + rows],
                                     ones[0:QK, 0:2], start=True, stop=True)
                for a in range(2):
                    mm = nc.tensor.matmul(pair(p)[0:QK, a, :], ones[0:QK, 0:QK],
                                          sq[0:QK, 0, a * HALF:(a + 1) * HALF], start=True, stop=True)
            mm.then_inc(jobs, 1)

        def act_m_part(name, at, n, buffers_read):
            p, job, _ = at
            kind, e = name[0], int(name[1])
            nc.scalar.wait_ge(jobs, job)
            if name == "V0":
                nc.scalar.wait_ge(na_sync.q_lo, 3 * PAIRS)
                nc.scalar.activation(val[0:META, 0, :], ps[0:META, 2 * p, :], ACT.Copy)
                nc.scalar.activation(val[:, 1, :], ps[:, 2 * p + 1, :], ACT.Copy).then_inc(free[p], 1)
            elif name == "V1":
                nc.scalar.activation(val[:, 2:4, :], ps[:, 2 * p:2 * p + 2, :], ACT.Copy).then_inc(free[p], 1)
            elif name == "V2":
                nc.scalar.activation(val[:, 4, :], ps[:, 2 * p, :], ACT.Copy).then_inc(free[p], 1)
                split_hi(C_V + 3, 0, job)
            elif kind == "k":
                nc.scalar.wait_ge(*buffers_read)
                nc.scalar.activation(m_k[NOPE:QK, e, :], rot_k[NOPE:QK, :], ACT.Copy)
                nc.scalar.activation(two(m_k[0:NOPE, e, :]), pair(p)[0:NOPE], ACT.Copy,
                                     scale=gain[0:NOPE, G_MK:G_MK + 1])
                nc.scalar.activation(two(sq[0:NOPE, 0, :]), pair(p)[0:NOPE], ACT.Square).then_inc(free[p], 1)
            elif kind == "q":
                nc.scalar.activation(two(m_q[:, e, :]), pair(p), ACT.Copy, scale=gain[:, G_MQ:G_MQ + 1])
                nc.scalar.activation(two(sq[0:QK, 1, :]), pair(p)[0:QK], ACT.Square).then_inc(free[p], 1)
            else:
                nc.scalar.activation(q_rms[:, 1:5, e], ps[:, 2 * p, STAT + 2:STAT + 10:2], ACT.Sqrt, bias=eps[:, 2:3])
                nc.scalar.activation(q_rms[0:META, 0, e:e + 1], ps[0:META, 2 * p, STAT:STAT + 1], ACT.Sqrt,
                                     bias=eps[0:META, 2:3])
                nc.scalar.wait_ge(rms_read, 2 + 2 * (PAIRS + 2 * n + e))
                nc.scalar.activation(two(rms[0:QK, :]), pair(p)[0:QK], ACT.Sqrt, bias=eps[0:QK, 0:1],
                                     scale=1.0 / QK).then_inc(free[p], 1)

        def dve_turn(x, done):
            rows = slice(NOPE, QK)
            dve.after(nc.vector.tensor_tensor(rstd[rows, :], x[QK:P, :], sin[QK:P, :], ALU.mult))
            dve.after(nc.vector.tensor_tensor(x[rows, :], x[rows, :], cos[rows, :], ALU.mult))
            nc.vector.tensor_tensor(x[rows, :], x[rows, :], rstd[rows, :], ALU.add).then_inc(done, 1)

        def dve_m_turn(at, n, e, shared):
            nc.vector.wait_ge(free[at[0]], at[2] + 1)
            if shared:
                nc.vector.wait_ge(m_key_normed, 2 * n + e)
            dve_turn(m_q[:, e, :], m_done)
            nc.vector.wait_ge(m_done, 2 * n + e + 1)

        def pool_key(n, e):
            nc.gpsimd.wait_ge(rms_read, 2 + 2 * PAIRS + 2 * (2 * n + e + 1))
            nc.gpsimd.tensor_tensor(m_k[0:QK, e, :], m_k[0:QK, e, :], rstd[0:QK, :], ALU.mult).then_inc(m_key_normed, 1)

        def act_up_hi(n):
            nc.scalar.wait_ge(up_loaded, 16 * (n + 1))
            nc.scalar.activation(up_hi[:], up_raw[:], ACT.Copy).then_inc(up_hi_done, 1)

        def dve_up_lo(n):
            nc.vector.wait_ge(up_hi_done, n + 1)
            nc.vector.tensor_tensor(up_lo[:], up_raw[:], up_hi[:], ALU.subtract).then_inc(up_split, 1)

        def pool_up_load(n, job):
            if not at_start(n):
                nc.gpsimd.wait_ge(jobs, job)
            nc.gpsimd.dma_start(up_raw[:], up_weights[n]).then_inc(up_loaded, 16)

        BEGIN = ("q", "k", "v", "st", "vt")

        def begin_at(j, b, name):
            k = BEGIN.index(name)
            return k % 4, j + 1 + k, b[k % 4] + k // 4

        def pe_begin(j, b):
            for k, name in enumerate(BEGIN):
                if name == "st":
                    nc.tensor.wait_ge(free[1], b[1] + 1)
                if name == "vt":
                    nc.tensor.wait_ge(free[2], b[2] + 1)
                pe_na_part(name, 0, PARTS.get(name, 1), begin_at(j, b, name), C_NA + k, 0)

        def act_begin(j, b):
            for k, name in enumerate(BEGIN):
                act_na_part(name, begin_at(j, b, name), C_NA + k, 0, 0, None)
                if name == "q":
                    for t in range(QL + KL):
                        nc.scalar.wait_ge(lat_normed, QL if t < QL else QL + KL)
                        nc.scalar.activation(lat_hi[:, t, :], lat[:, t, :], ACT.Copy).then_inc(lat_hi_done, 1)

        def act_rotary_squares(j_stat):
            nc.scalar.wait_ge(jobs, j_stat)
            nc.scalar.activation(sq[NOPE:QK, 0, :], rot_sq[NOPE:QK, :], ACT.Copy)

        def dve_begin(j, b):
            split_lo(C_NA + 3, 0)
            for t in range(QL + KL):
                nc.vector.wait_ge(lat_hi_done, t + 1)
                nc.vector.tensor_tensor(lat_lo[:, t, :], lat[:, t, :], lat_hi[:, t, :],
                                        ALU.subtract)
            for k in (1, 2):
                split_lo(C_NA + 3 + k, 0)
            for second in (False, True):
                dve_na_key(begin_at(j, b, "st"), 0, second)
            dve_turn(rot_k, rot_ready)
            nc.vector.wait_ge(rot_ready, 1)

        class Sync:

            def __init__(self, name):
                self.q_hi, self.q_lo = sem(f"{name}_split_hi"), sem(f"{name}_split_lo")
                self.bias = sem(f"{name}_exp_bias")
                self.exp = sem(f"{name}_exp")
                self.prob = sem(f"{name}_prob")
                self.p_hi = sem(f"{name}_p_hi")
                self.scale = sem(f"{name}_scale")

        na_sync, m_sync = Sync("na"), Sync("mla")

        def steps(eng, body):
            body(0)
            with eng.Fori(1, PAIRS - 1) as i:
                body(i)
            body(PAIRS - 1)

        def pair_of(i):
            return i if isinstance(i, int) else 1

        def na_width(x):
            a, e = NA_KEYS[x]
            return META + P * (e - a)

        def splits_per_step(mla):
            return 5 if mla else 3

        def scores_at(mla, x, p):
            return pair(p)[0:block_at(x)[1]] if mla else ps[0:block_at(x)[1], 2 * p, 0:na_width(x)]

        def prob_at(mla, u, x):
            n = block_at(x)[1]
            return two(prob[0:n, PROB[u], :]) if mla else prob[0:n, PROB[u], 0:na_width(x)]

        def pe_attention(mla, y, plan):
            def scores(u, i):
                e, x = divmod(u, 5)
                q0, n = block_at(x)
                p = S_PAIR
                wait(nc.tensor, free[p], plan.prior(f"S{u}", i))
                if mla and x == 0:
                    nc.tensor.wait_ge(y.q_lo, 2 + 3 * e + 5 * i)
                elif u == 0:
                    nc.tensor.wait_ge(y.q_lo, 2 + 3 * i)
                if x == 0:
                    nc.tensor.sem_inc(small_turn, 1)
                qh, ql, kh, kl = m_s if mla else na_s
                rows = slice(0, QK) if mla else slice(HD * e, HD * e + HD)
                if mla:
                    parts = [(pair(p)[0:n, a, :], a * HALF, HALF) for a in range(2)]
                else:
                    a, z = NA_KEYS[x]
                    parts = [(ps[0:n, 2 * p, 0:META], 0, META)]
                    if x:
                        parts.append((ps[0:n, 2 * p, META:na_width(x)], META + P * a, P * (z - a)))
                for dst, k0, w in parts:
                    for k, (l, r) in enumerate(((qh, kh), (qh, kl), (ql, kh))):
                        mm = nc.tensor.matmul(dst, l[rows, q0:q0 + n], r[rows, k0:k0 + w], start=k == 0, stop=k == 2)
                mm.then_inc(jobs, 1)

            def transposes(name, i, step):
                u = int(name[1])
                x = u % 5
                n, p = block_at(x)[1], T_PAIR
                nc.tensor.wait_ge(y.prob, UNITS * step + u + 1)
                wait(nc.tensor, free[p], plan.prior(name, i))
                if x == 0:
                    nc.tensor.sem_inc(small_turn, 1)
                a, z = (0, 4) if mla else NA_KEYS[x]
                src = prob[0:n, PROB[u], :]
                for k in range(z - a):
                    nc.tensor.transpose(ps[:, 2 * p, P * k:P * k + n], src[:, META + P * k:META + P * (k + 1)],
                                        mat[0:n, 0, 0:n])
                nc.tensor.transpose(ps[0:META, 2 * p + 1, 0:n], src[:, 0:META], mat[0:n, 0, 0:n]).then_inc(jobs, 1)

            def values(name, i, step):
                e = 1 if name == "PVp" else 0
                last = "T9p" if e else "T4"
                nc.tensor.wait_ge(free[psum_pair(last)], plan.prior(last, i) + 1)
                wait(nc.tensor, free[1], plan.prior(name, i))
                if not e:
                    nc.tensor.wait_ge(y.q_lo, splits_per_step(mla) * i + 3)
                m = P if e else HD
                if mla:
                    groups = [(2, 0, 272, [(a, 0, 272) for a in range(5)]),
                              (3, 272, 256, [(a, 272, 256) for a in range(5)])]
                else:
                    groups = [(2, META, SEQ, [(0, META, SEQ)] + [
                        (1 + a, META + P * lo, P * (hi - lo)) for a, (lo, hi) in enumerate(NA_KEYS[1:])]),
                        (3, 0, META, [(0, 0, META)])]
                for bank, base, _, parts in groups:
                    for k, (a, q0, w) in enumerate(parts):
                        rows = slice(0, META if a == 0 else P)
                        hi, lo = (pm_hi[:].unsqueeze(1), pm_lo[:].unsqueeze(1)) if a == 0 else (p_hi, p_lo)
                        for t, (l, r) in enumerate(((v_hi, hi), (v_hi, lo), (v_lo, hi))):
                            mm = nc.tensor.matmul(ps[0:m, bank, q0 - base:q0 - base + w], l[rows, a, 0:m],
                                                  r[rows, max(a - 1, 0), q0:q0 + w], start=k == 0 and t == 0,
                                                  stop=k == len(parts) - 1 and t == 2)
                mm.then_inc(jobs, 1)

            def step(i):
                for name, lo, hi in plan.work[pair_of(i)]:
                    before = i - 1 if name[-1] == "p" else i
                    if name[0] == ".":
                        continue
                    if name[0] == "S":
                        scores(int(name[1]), i)
                    elif name[0] == "T":
                        transposes(name, i, before)
                    elif name[:2] == "PV":
                        values(name, i, before)
                    elif name in PARTS or name in ("st", "vt"):
                        if name in ("st", "vt"):
                            of = plan.at("k" if name == "st" else "v", i)
                            nc.tensor.wait_ge(free[of[0]], of[2] + 1)
                            nc.tensor.sem_inc(small_turn, 1)
                        piece = plan.piece(name, i) if name in PARTS else (0, 0)
                        pe_na_part(name, lo, hi, plan.at(name, i), *piece)
                    else:
                        pe_m_part(name, plan.at(name, i), i + 1 if mla else 0)

            steps(nc.tensor, step)
            for name in ("T8p", "T9p"):
                transposes(name, PAIRS, PAIRS - 1)
            values("PVp", PAIRS, PAIRS - 1)

        def split_q_k(mla, e):
            if mla:
                return [(x[0:QK, e, :], m_s[k][0:QK, :], m_s[k + 1][0:QK, :]) for k, x in ((0, m_q), (2, m_k))]
            return [(x[:], na_s[k][:], na_s[k + 1][:]) for k, x in ((0, na_q), (2, na_k))]

        def next_free(mla, y, name, i):
            if not mla:
                return y.q_lo, 3 * i + 2
            return y.q_lo, 5 * i + (5 if name[-1] == "1" else 2)

        def act_attention(mla, y, plan):
            def split(e, i):
                if e:
                    nc.scalar.wait_ge(jobs, plan.job("S4", i))
                elif not at_start(i):
                    nc.scalar.wait_ge(jobs, plan.job_before("S9", i))
                if mla:
                    nc.scalar.wait_ge(m_key_normed, 2 * i + e + 1)
                    nc.scalar.wait_ge(m_done, 2 * i + e + 1)
                else:
                    nc.scalar.wait_ge(na_k_ready, i + 1)
                for src, hi, _ in split_q_k(mla, e):
                    nc.scalar.activation(hi, src, ACT.Copy).then_inc(y.q_hi, 1)

            def exp(u, i):
                e, x = divmod(u, 5)
                n = block_at(x)[1]
                p = S_PAIR
                nc.scalar.wait_ge(y.bias, UNITS * i + u + 1)
                if mla:
                    prob_free(nc.scalar, plan, u, i)
                    nc.scalar.activation(prob_at(mla, u, x), scores_at(mla, x, p), ACT.Exp,
                                         bias=exp_bias[0:n, u:u + 1], scale=q_scale[0:n, x, e:e + 1],
                                         accum_out=exp_sum[0:n, u:u + 1]).then_inc(free[p], 1)
                else:
                    nc.scalar.activation(prob_at(mla, u, x), prob_at(mla, u, x), ACT.Exp, bias=neg_max[0:n, u:u + 1],
                                         accum_out=exp_sum[0:n, u:u + 1]).then_inc(y.exp, 1)

            def hi_of_transposed(name, i, step):
                u = int(name[1])
                x = u % 5
                (q0, n), p = block_at(x), T_PAIR
                nc.scalar.wait_ge(jobs, plan.job(name, i))
                a, z = (0, 4) if mla else NA_KEYS[x]
                if z > a:
                    nc.scalar.activation(p_hi[:, a:z, q0:q0 + n], blocks(p, z - a, n), ACT.Copy)
                nc.scalar.activation(pm_hi[:, q0:q0 + n], ps[0:META, 2 * p + 1, 0:n],
                                     ACT.Copy).then_inc(y.p_hi, 1)

            def output(name, i, pair_no):
                e = 1 if name == "PVp" else 0
                rows = slice(HD * e, HD * e + HD)
                nc.scalar.wait_ge(jobs, plan.job(name, i))
                t = pair_no + 4 if mla else pair_no
                cuts = ((2, 0, 272), (3, 272, 256)) if mla else ((2, META, SEQ), (3, 0, META))
                for k, (bank, q0, w) in enumerate(cuts):
                    ins = nc.scalar.activation(o[rows, ds(t), q0:q0 + w].rearrange("p a t -> p (a t)"),
                                               ps[rows, bank, 0:w], ACT.Copy)
                ins.then_inc(free[1], 1)

            def step(i):
                split(0, i)
                if mla and isinstance(i, int) and i == PAIRS - 1:
                    nc.scalar.wait_ge(gate_stored, 16 * plan.gate("g1", i))
                for name, lo, hi in plan.work[pair_of(i)]:
                    before = i - 1 if name[-1] == "p" else i
                    if name == ".vs":
                        if not at_start(i):
                            nc.scalar.wait_ge(jobs, plan.job("PVp", i))
                        nc.scalar.activation(v_hi[:], val[:, :, ds(P * i, P)], ACT.Copy).then_inc(y.q_hi, 1)
                    elif name == ".s":
                        split(1, i)
                    elif name == ".u" and mla:
                        act_up_hi(i + 1)
                    elif name == ".u":
                        nc.scalar.wait_ge(rot_ready, 1)
                        act_rotary_squares(plan.job("st", PAIRS - 2))
                        nc.scalar.wait_ge(gate_stored, 16 * plan.after()[3])
                        act_up_hi(0)
                    elif name[0:2] in (".a", ".b", ".n", ".t", ".e", ".f"):
                        continue
                    elif name[:2] == ".g":
                        last = isinstance(i, int) and i == PAIRS - 1
                        act_gate(name[1:], plan, i, gate_m if mla and not last else gate_na)
                    elif name in (".q", ".k", ".st", ".v", ".vt"):
                        act_na_part(name[1:], plan.at(name[1:], i),
                                    *(plan.piece(name[1:], i) if name[1:] in PARTS else (0, 0)), i + 1,
                                    next_free(mla, y, name, i))
                    elif name[0] == ".":
                        act_m_part(name[1:], plan.at(name[1:], i), i + 1 if mla else 0, next_free(mla, y, name, i))
                    elif name[0] == "S":
                        exp(int(name[1]), i)
                    elif name[0] == "T":
                        hi_of_transposed(name, i, before)
                    elif name[:2] == "PV":
                        output(name, i, before)

            steps(nc.scalar, step)
            hi_of_transposed("T8p", PAIRS, PAIRS - 1)
            hi_of_transposed("T9p", PAIRS, PAIRS - 1)
            output("PVp", PAIRS, PAIRS - 1)

        def prob_free(eng, plan, u, i):
            user = PROB_USER[u]
            if user in ("T6", "T7"):
                if not at_start(i):
                    eng.wait_ge(jobs, plan.job_before(user, i))
            elif user[-1] != "p" or not at_start(i):
                eng.wait_ge(jobs, plan.job(user, i))

        def blocks(p, count, n):
            return ps[:, 2 * p, 0:P * count].rearrange("p (k q) -> p k q", q=P)[:, :, 0:n]

        def dve_attention(mla, y, plan):
            def split(e, i):
                first = splits_per_step(mla) * i + 3 * e
                for k, (src, hi, lo) in enumerate(split_q_k(mla, e)):
                    nc.vector.wait_ge(y.q_hi, first + k + 1)
                    nc.vector.tensor_tensor(lo, src, hi, ALU.subtract).then_inc(y.q_lo, 1)

            def top(u, i):
                e, x = divmod(u, 5)
                n = block_at(x)[1]
                p = S_PAIR
                nc.vector.wait_ge(jobs, plan.job(f"S{u}", i))
                if mla:
                    dve.after(nc.vector.tensor_reduce(neg_max[0:n, u:u + 1], scores_at(mla, x, p), AX.XY, ALU.max,
                                                      negate=True))
                    nc.vector.tensor_tensor(exp_bias[0:n, u:u + 1], neg_max[0:n, u:u + 1],
                                            q_scale[0:n, x, e:e + 1], ALU.mult).then_inc(y.bias, 1)
                    return
                prob_free(nc.vector, plan, u, i)
                w = na_width(x)
                if x == 0:
                    nc.vector.tensor_scalar(prob[0:n, PROB[u], 0:w], ps[0:n, 2 * p, 0:w], q_scale[0:n, x, e:e + 1],
                                            None, ALU.mult).then_inc(free[p], 1)
                else:
                    if x == 1:
                        nc.vector.wait_ge(bias_ready, 3 * (2 * i + e) + 3)
                    at_bias = (0, 0, META + 2 * P, META + 2 * P, 2 * META + 5 * P)[x]
                    nc.vector.scalar_tensor_tensor(prob[:, PROB[u], 0:w], ps[:, 2 * p, 0:w], q_scale[:, x, e:e + 1],
                                                   na_bias[:, e, at_bias:at_bias + w], ALU.mult,
                                                   ALU.add).then_inc(free[p], 1)
                nc.vector.wait_ge(free[p], plan.prior(f"S{u}", i) + 1)
                nc.vector.tensor_reduce(neg_max[0:n, u:u + 1], prob[0:n, PROB[u], 0:w], AX.X, ALU.max,
                                        negate=True).then_inc(y.bias, 1)

            def normalise(u, i):
                x = u % 5
                n = block_at(x)[1]
                if mla:
                    nc.vector.wait_ge(free[S_PAIR], plan.prior(f"S{u}", i) + 1)
                else:
                    nc.vector.wait_ge(y.exp, UNITS * i + u + 1)
                dve.after(nc.vector.reciprocal(exp_rec[0:n, u:u + 1], exp_sum[0:n, u:u + 1]))
                w = T if mla else na_width(x)
                nc.vector.tensor_scalar(prob[0:n, PROB[u], 0:w], prob[0:n, PROB[u], 0:w], exp_rec[0:n, u:u + 1], None,
                                        ALU.mult).then_inc(y.prob, 1)

            def lo_of_transposed(name, i, step):
                u = int(name[1])
                x = u % 5
                (q0, n), p = block_at(x), T_PAIR
                nc.vector.wait_ge(y.p_hi, UNITS * step + u + 1)
                a, z = (0, 4) if mla else NA_KEYS[x]
                if z > a:
                    nc.vector.tensor_tensor(p_lo[:, a:z, q0:q0 + n], blocks(p, z - a, n),
                                            p_hi[:, a:z, q0:q0 + n], ALU.subtract)
                nc.vector.tensor_tensor(pm_lo[:, q0:q0 + n], ps[0:META, 2 * p + 1, 0:n],
                                        pm_hi[:, q0:q0 + n], ALU.subtract).then_inc(free[p], 1)

            def in_order(work):
                order, later = [], []
                for name, _, _ in work:
                    if name[0] == "." and (name[1:] in PARTS or name == ".V2"):
                        later.append(name)
                        continue
                    order.append(name)
                    if name[0] == "S":
                        order, later = order + later, []
                return order + later

            def step(i):
                if not at_start(i):
                    normalise(9, i - 1)
                nc.vector.reciprocal(q_scale[:], q_rms[:]).then_inc(y.scale, 1)
                nc.vector.wait_ge(y.scale, i + 1)
                split(0, i)
                for name in in_order(plan.work[pair_of(i)]):
                    before = i - 1 if name[-1] == "p" else i
                    if name[0] == "S":
                        u = int(name[1])
                        top(u, i)
                        if u > 0:
                            normalise(u - 1, i)
                    elif name == ".u":
                        dve_up_lo(i + 1 if mla else 0)
                    elif name in (".e", ".f"):
                        dve_m_key(na_plan.at("z1", PAIRS - 1), 0, 1, name == ".f", False)
                    elif name == ".vs" and not mla:
                        nc.vector.wait_ge(y.q_hi, splits_per_step(mla) * i + 3)
                        nc.vector.tensor_tensor(v_lo[:], val[:, :, ds(P * i, P)], v_hi[:],
                                                ALU.subtract).then_inc(y.q_lo, 1)
                    elif name == ".vs":
                        continue
                    elif name == ".s":
                        nc.vector.wait_ge(y.q_lo, 5 * i + 3)
                        split(1, i)
                    elif name in (".na", ".nb"):
                        dve_na_key(plan.at("st", i), i + 1, name == ".nb")
                    elif name[:2] == ".g":
                        split_lo(*ahead(plan.piece(name[1:], i)))
                    elif name[:2] in (".a", ".b"):
                        dve_m_key(plan.at("z" + name[2], i), i + 1 if mla else 0, int(name[2]), name[1] == "b", mla)
                    elif name in (".q", ".k", ".st", ".v", ".vt"):
                        if name[1:] in PARTS:
                            split_lo(*ahead(plan.piece(name[1:], i)))
                    elif name[0:2] == ".t":
                        dve_m_turn(plan.at("q" + name[2], i), i + 1 if mla else 0, int(name[2]), mla)
                    elif name == ".V2":
                        split_lo(C_V + SLOTS, 0)
                    elif name[0] == ".":
                        continue
                    elif name[0] == "T":
                        lo_of_transposed(name, i, before)
                    elif name[:2] == "PV":
                        continue

            per = 2 * UNITS + 4 if mla else UNITS
            dve.enter(per - 1, 0)
            step(0)
            dve.leave(1)
            with nc.vector.Fori(1, PAIRS - 1) as i:
                dve.enter(per, i - 1)
                step(i)
            dve.leave(PAIRS - 2)
            step(PAIRS - 1)
            normalise(9, PAIRS - 1)
            lo_of_transposed("T8p", PAIRS, PAIRS - 1)
            lo_of_transposed("T9p", PAIRS, PAIRS - 1)

        def pool_attention(y, plan):
            def step(i):
                if not isinstance(i, int):
                    pool_up_load(i + 1, plan.job_before("q1", i))
                for name, _, _ in plan.work[pair_of(i)]:
                    if name == ".vs":
                        nc.gpsimd.wait_ge(y.q_hi, splits_per_step(True) * i + 3)
                        nc.gpsimd.tensor_tensor(v_lo[:], val[:, :, ds(P * i, P)], v_hi[:],
                                                ALU.subtract).then_inc(y.q_lo, 1)
                    elif name[:2] == ".b":
                        pool_key(i + 1, int(name[2]))

            step(0)
            with nc.gpsimd.Fori(1, PAIRS - 1) as i:
                step(i)
            step(PAIRS - 1)

        def pool_na_bias():
            def head(e, i):
                for r in range(ROWS):
                    if not (at_start(i) and e == 0):
                        if r == 0:
                            nc.gpsimd.wait_ge(bias_ready, 3 * (2 * i + e))
                    src = bias[ds(2 * i + e), :, :, (ROWS - 1 - r) * BLK:(2 * ROWS - 1 - r) * BLK]
                    nc.gpsimd.dma_start(raw_bias[BLK * r:BLK * (r + 1), :].rearrange("p (a k) -> p a k", a=3),
                                        src.rearrange("h c a k -> (h c) a k")).then_inc(bias_loaded, 16)
                if not at_start(i):
                    nc.gpsimd.wait_ge(na_sync.bias, UNITS * (i - 1) + 5 * e + 5)
                nc.gpsimd.wait_ge(bias_loaded, 16 * ROWS * (2 * i + e + 1))
                m0, b0 = 0, META
                for lo, hi in ((1, 3), (0, 3), (0, 2)):
                    w = P * (hi - lo)
                    nc.gpsimd.tensor_tensor(na_bias[:, e, b0:b0 + w], raw_bias[:, P * lo:P * hi],
                                            na_mask[:, m0:m0 + w], ALU.add).then_inc(bias_ready, 1)
                    m0, b0 = m0 + w, b0 + w + META

            def step(i):
                head(0, i)
                head(1, i)

            nc.gpsimd.wait_ge(pool_ready, 3)
            nc.gpsimd.wait_ge(load_c, 16 * CONSTS)
            step(0)
            with nc.gpsimd.Fori(1, PAIRS) as i:
                step(i)

        O_ORDER = (4, 5, 6, 7, 0, 1, 2, 3)

        def pe_merge(j, b):
            for m in range(DK):
                c = C_BRANCH + m
                nc.tensor.wait_ge(lo_done, c + 1)
                for e in range(2):
                    p = 2 * (m % 2) + e
                    nc.tensor.wait_ge(free[p], b[p] + m // 2)
                    for t in range(4):
                        if m == 0:
                            nc.tensor.wait_ge(o_split, 4 * e + t + 1)
                        k = O_ORDER[4 * e + t]
                        mm = three_passes(pair(p), weight(c, 4 * e + t), (o_hi[:, k, :], o_lo[:, k, :]),
                                          t == 0, t == 3)
                    mm.then_inc(jobs, 1)

        def pool_gate_load(j_free):
            for m in range(DK):
                nc.gpsimd.wait_ge(gate_stored, 32 * (m + 1))
                if m < 3:
                    nc.gpsimd.wait_ge(jobs, j_free[m])
                else:
                    nc.gpsimd.wait_ge(g_split, m - 2)
                nc.gpsimd.dma_start(gated[m % 3][:], gates[2 * m:2 * m + 2].rearrange("a p t -> p a t")).then_inc(
                    gate_loaded[m % 3], 16)

        def act_merge(j, b):
            def sigmoid(m):
                nc.scalar.wait_ge(gate_loaded[m % 3], 16 * (m // 3 + 1))
                nc.scalar.activation(gated[m % 3][:], gated[m % 3][:], ACT.Sigmoid).then_inc(gate_ready, 1)

            nc.scalar.wait_ge(free[1], b[1])
            for t in O_ORDER:
                nc.scalar.activation(o_hi[:, t, :], o[:, t, :], ACT.Copy).then_inc(o_hi_done, 1)
            sigmoid(0)
            for m in range(DK):
                if m + 1 < DK:
                    sigmoid(m + 1)
                split_hi(C_BRANCH + 3 + m, 0, j + 2 + 2 * m)
                nc.scalar.wait_ge(g_ready, m + 1)
                nc.scalar.activation(g_hi[:, m, :], gated[m % 3][:, 0, :], ACT.Copy).then_inc(g_hi_done, 1)

        def dve_merge(j, b):
            for n, t in enumerate(O_ORDER):
                nc.vector.wait_ge(o_hi_done, n + 1)
                nc.vector.tensor_tensor(o_lo[:, t, :], o[:, t, :], o_hi[:, t, :], ALU.subtract).then_inc(o_split, 1)
            for m in range(DK):
                both, p = gated[m % 3], 2 * (m % 2)
                nc.vector.wait_ge(gate_ready, m + 1)
                for e in range(2):
                    nc.vector.wait_ge(jobs, j + 1 + e + 2 * m)
                    nc.vector.tensor_tensor(two(both[:, e, :]), pair(p + e), two(both[:, e, :]),
                                            ALU.mult).then_inc(free[p + e], 1)
                nc.vector.wait_ge(free[p], b[p] + 1 + m // 2)
                nc.vector.wait_ge(free[p + 1], b[p + 1] + 1 + m // 2)
                nc.vector.tensor_tensor(both[:, 0, :], both[:, 0, :], both[:, 1, :], ALU.add).then_inc(g_ready, 1)
                split_lo(C_BRANCH + 3 + m, 0)
                nc.vector.wait_ge(g_hi_done, m + 1)
                nc.vector.tensor_tensor(g_lo[:, m, :], both[:, 0, :], g_hi[:, m, :], ALU.subtract).then_inc(g_split, 1)

        def pe_out(j, b):
            def part(m, tiles):
                c, p = C_OUT + m, m % 4
                if tiles[0] == 0:
                    nc.tensor.wait_ge(lo_done, c + 1)
                    nc.tensor.wait_ge(free[p], b[p] + m // 4)
                for t in tiles:
                    if m == 0:
                        nc.tensor.wait_ge(g_split, t + 1)
                    mm = three_passes(pair(p), weight(c, t), (g_hi[:, t, :], g_lo[:, t, :]), t == 0, t == DK - 1)
                if tiles[-1] == DK - 1:
                    mm.then_inc(jobs, 1)

            for m in (0, 1):
                part(m, range(DK - 1))
            for m in (0, 1):
                part(m, [DK - 1])
            for m in range(2, DK):
                part(m, range(DK))

        def act_out(j, b):
            for m in range(DK - 1):
                split_hi(C_OUT + 3 + m, 0, j + 1 + m)

        def dve_out(j, b):
            for m in range(DK):
                nc.vector.wait_ge(jobs, j + 1 + m)
                nc.vector.tensor_tensor(two(h[:, m, :]), pair(m % 4), two(h[:, m, :]), ALU.add).then_inc(free[m % 4], 1)
                if m < DK - 1:
                    split_lo(C_OUT + 3 + m, 0)

        def more(b, *n):
            return [x + y for x, y in zip(b, n)]

        b1, j1 = [0, 0, 1, 0], 1
        b2, j2 = after_ffn(b1, j1)
        b_lat, j_lat = more(b2, 0, 0, 1, 0), j2 + 1
        b_na, j_na = more(b_lat, 2, 2, 2, 2), j_lat + 8
        na_plan = Plan(j_na + 5, more(b_na, 2, 1, 1, 1), C_STEPS, 0, NA_FIRST, NA_STEP, NA_LAST)
        m_plan = Plan(*(na_plan.after()[k] for k in (1, 0, 2, 3)), M_FIRST, M_STEP, M_LAST)
        b_mrg, j_mrg, c_mrg, n_gates = m_plan.after()
        assert (c_mrg, n_gates) == (C_BRANCH, 2 * DK)
        b_out, j_out = more(b_mrg, DK // 2, DK // 2, DK // 2, DK // 2), j_mrg + 2 * DK
        b3, j3 = more(b_out, 2, 2, 2, 2), j_out + DK
        b4, j4 = more(b3, 0, 0, 1, 0), j3 + 1

        block = ctx.enter_context(nc.Block())

        @block.sync
        def _(sp):
            def load_piece(c, i=0):
                s = c % SLOTS
                wait(sp, lo_done, c - 2 + 3 * i)
                piece = weights[ds(c + 3 * i)].rearrange("a p e -> (a p) e")
                sp.dma_start(w_raw[:, s, :], piece).then_inc(loaded[s], 16)

            for m in range(DK):
                sp.dma_start(h[:, m, :], xT[m]).then_inc(load_x[m], 16)
            sp.dma_start(gain[:], gains).then_inc(load_gain, 16)
            for c in range(SLOTS):
                load_piece(c)
            sp.dma_start(mat[:], mats).then_inc(load_c, 16)
            sp.dma_start(cos[NOPE:QK, :], rope[0]).then_inc(load_c, 16)
            sp.dma_start(sin[QK:P, :], rope[1]).then_inc(load_c, 16)
            sp.dma_start(na_mask[:], mask).then_inc(load_c, 16)
            with sp.Fori(0, N_PIECES // SLOTS - 1) as i:
                for c in range(SLOTS, 2 * SLOTS):
                    load_piece(c, i)
            for c in range(N_PIECES // SLOTS * SLOTS, N_PIECES):
                load_piece(c)
            for m, done in enumerate(ffn_h_ready(b4)):
                sp.wait_ge(*done)
                sp.dma_start(out[m], h[:, m, META:]).then_inc(stored, 16)
            sp.wait_ge(stored, 16 * DK)

        @block.tensor
        def _(pe):
            pe.wait_ge(const_ready, 4)
            pe_norm_sums(0, 2, 0)
            pe_ffn(0, 0, C_FFN1, b1)
            pe_norm_sums(1, 2, b2[2])
            pe.wait_ge(load_c, 16 * CONSTS)
            pe_latents(j_lat, b_lat)
            pe_begin(j_na, b_na)
            pe_attention(False, na_sync, na_plan)
            pe_attention(True, m_sync, m_plan)
            pe_merge(j_mrg, b_mrg)
            pe_out(j_out, b_out)
            pe_norm_sums(2, 2, b3[2])
            pe_ffn(1, 2, C_FFN2, b4)

        @block.scalar
        def _(act):
            act.wait_ge(const_ready, 4)
            act_norm_squares(0, 2, 1, [(load_x[m], 16) for m in range(DK)])
            for c in range(SLOTS):
                split_hi(c, 0, 0)
            act_norm_hi(0)
            act_ffn(C_FFN1, b1, j1, 0)
            split_hi(C_LAT + 1, 0, down_tile_job(j1, DK - 1, FC - 1))
            act_norm_squares(1, 2, j2 + 1, ffn_h_ready(b1))
            split_hi(C_LAT + 2, 0, down_tile_job(j1, DK - 1, FC))
            act_norm_hi(1)
            act_latents(j_lat, b_lat)
            act_begin(j_na, b_na)
            act_attention(False, na_sync, na_plan)
            act_attention(True, m_sync, m_plan)
            act_merge(j_mrg, b_mrg)
            act_out(j_out, b_out)
            act_norm_squares(2, 2, j3 + 1, [(free[m % 4], b_out[m % 4] + m // 4 + 1) for m in range(DK)])
            split_hi(C_FFN2 + 2, 0, j_out + DK)
            act_norm_hi(2)
            act_ffn(C_FFN2, b4, j4, 1)

        @block.vector
        def _(eng):
            eng.memset(ones[:], 1.0).then_inc(const_ready, 1)
            for k, factor in enumerate((1, HD, QK)):
                eng.memset(eps[:, k:k + 1], EPS * factor).then_inc(const_ready, 1)
            eng.wait_ge(load_gain, 16)
            dve_norm(0, 2, 0, G_FFN1, split_first=(0, 1))
            split_lo(2, 0)
            eng.wait_ge(load_c, 16 * CONSTS)
            dve_ffn(C_FFN1, b1, j1, 0)
            split_lo(C_LAT + 1, 0)
            dve_norm(1, 2, b2[2], G_MIX)
            split_lo(C_LAT + 2, 0)
            dve_latents(j_lat, b_lat)
            eng.wait_ge(pool_ready, 3)
            dve_begin(j_na, b_na)
            dve_attention(False, na_sync, na_plan)
            dve_attention(True, m_sync, m_plan)
            dve_merge(j_mrg, b_mrg)
            dve_out(j_out, b_out)
            dve_norm(2, 2, b3[2], G_FFN2)
            split_lo(C_FFN2 + 2, 0)
            dve_ffn(C_FFN2, b4, j4, 1)

        @block.gpsimd
        def _(gp):
            gp.memset(val[:, 0, :], 0.0).then_inc(pool_ready, 1)
            gp.memset(na_bias[:], 0.0).then_inc(pool_ready, 1)
            gp.memset(q_rms[:], 1.0).then_inc(pool_ready, 1)
            pool_up_load(0, 0)
            pool_ffn(0)
            pool_na_bias()
            pool_up_load(1, na_plan.job("q1", PAIRS - 1))
            pool_attention(m_sync, m_plan)
            pool_gate_load((m_plan.job("z1", PAIRS - 2), m_plan.job("T7", PAIRS - 1), m_plan.job("T9p", PAIRS)))
            pool_ffn(1)


def token_order():
    real = np.arange(SEQ).reshape(8, 4, 16).transpose(1, 0, 2).reshape(-1)
    return real


def column_pieces(w):
    n = w.shape[1] // P
    return w.reshape(DK, P, n, P).transpose(2, 1, 0, 3).reshape(n, P, PIECE)


def ffn_pieces(gate, up, down):
    g, u, d = column_pieces(gate), column_pieces(up), down.reshape(FC, P, D)
    order = [g[0], u[0]]
    for i in range(1, FC):
        order += [g[i], u[i], d[i - 1]]
    return order + [d[FC - 1]]


SWAP = (np.arange(ROPE) + ROPE // 2) % ROPE


def up_pieces(a):
    uk = a["mla_w_ukv"][0].reshape(KL, P, PAIRS, 2, 2, NOPE)[:, :, :, :, 0]
    uq = a["mla_w_uq"][0].reshape(QL, P, PAIRS, 2, QK)
    uq = np.concatenate([uq, uq[..., NOPE:][..., SWAP]], 4)
    return np.ascontiguousarray(np.concatenate([
        uk.transpose(2, 1, 0, 3, 4).reshape(PAIRS, P, -1), uq.transpose(2, 1, 0, 3, 4).reshape(PAIRS, P, -1)], 2))


def mixer_pieces(a):
    w = a["w_in"][0]
    lat, na, gates = w[:, :640], w[:, 672:2208], w[:, 2208:]
    rot = np.zeros((D, P), np.float32)
    rot[:, NOPE:QK] = w[:, 640:672]
    rot[:, QK:] = w[:, 640:672][:, SWAP]
    pieces = [column_pieces(rot), column_pieces(lat)]
    q, k, v = (column_pieces(na[:, 512 * n:512 * n + 512]) for n in range(3))
    ukv = a["mla_w_ukv"][0].reshape(KL, P, HEADS, 2, NOPE)[:, :, :, 1]
    values = ukv.transpose(1, 0, 2, 3).reshape(1, P, PIECE)
    gate = np.stack([column_pieces(gates[:, :D]), column_pieces(gates[:, D:])], 1).reshape(-1, P, PIECE)
    queue = {"q": iter(q), "k": iter(k), "v": iter(v), "g": iter(gate), "V": iter(values)}
    pieces.append(np.stack([next(queue[n[0]]) for n in ["q", "k", "v"] + STREAM]))
    pieces.append(column_pieces(np.concatenate([a["w_branch_a"][0], a["w_branch_b"][0]])))
    pieces.append(column_pieces(a["w_out"][0]))
    return np.concatenate(pieces)


def gain_columns(a):
    whole = [a[n][0].reshape(-1, P) for n in ("ffn1_norm", "mix_norm", "ffn2_norm", "mla_q_a_norm", "mla_kv_a_norm")]
    heads = [np.tile(a[n][0], 2)[None] for n in ("na_q_head_norm", "na_k_head_norm")]
    heads += [np.concatenate([a[n][0], a[n][0][NOPE:][SWAP]])[None] for n in ("mla_q_head_norm", "mla_k_head_norm")]
    return np.ascontiguousarray(np.concatenate(whole + heads).T)


def constant_matrices():
    m = np.zeros((P, 2, P), np.float32)
    m[:, 0] = np.eye(P)
    m[:HD, 1, :HD] = m[HD:, 1, HD:] = 1
    return m


def rotary_tables(real):
    pos = np.concatenate([np.arange(META), META + real]).astype(np.float32)
    half = ROPE // 2
    inv = np.float32(10000.0) ** (-np.arange(half, dtype=np.float32) / half)
    angle = inv[:, None] * pos[None]
    cos, sin = np.cos(angle), np.sin(angle)
    return np.stack([np.concatenate([cos, cos]), np.concatenate([-sin, sin])]).astype(np.float32)


def window_mask():
    parts = []
    for x in (1, 2, 4):
        lo, hi = NA_KEYS[x]
        col = BLK * (x - 1) + np.arange(BLK)
        start = np.clip(col - BLK // 2, 0, 4 * BLK - BLK)
        key = BLK * lo + np.arange(BLK * (hi - lo))
        inside = (key[None] >= start[:, None]) & (key[None] < start[:, None] + BLK)
        m = np.where(inside, 0, NEG).reshape(1, BLK, hi - lo, 1, BLK)
        parts.append(np.broadcast_to(m, (ROWS, BLK, hi - lo, ROWS, BLK)).reshape(P, -1))
    return np.concatenate(parts, 1).astype(np.dtype("bfloat16"))


def bias_diagonals(rel):
    heads, rows, reach = rel.shape
    g = np.zeros((heads, BLK, rows, 3 * BLK), np.float32)
    for c in range(BLK):
        g[:, c, :, c + 1:c + 1 + reach] = rel
    return np.ascontiguousarray(g.reshape(heads, BLK, rows, 3, BLK).transpose(0, 1, 3, 2, 4)).reshape(
        heads, BLK, 3, rows * BLK)


def kernel(**inputs):
    import concourse.bacc as bacc
    from concourse.bass_utils import run_bass_kernel_spmd

    a = {k: np.asarray(v) for k, v in inputs.items()}
    real = token_order()
    x = np.concatenate([a["meta_tokens"], a["x"][0][real]])
    ffn1, ffn2 = (ffn_pieces(*(a[f"ffn{n}_w_{k}"][0] for k in ("gate", "up", "down"))) for n in (1, 2))
    arrays = {
        "weights": np.concatenate([np.stack(ffn1), mixer_pieces(a), np.stack(ffn2)]),
        "up_weights": up_pieces(a),
        "xT": np.ascontiguousarray(x.T.reshape(DK, P, T)),
        "gains": gain_columns(a),
        "mats": constant_matrices(),
        "rope": rotary_tables(real),
        "mask": window_mask(),
        "bias": bias_diagonals(a["na_rel_bias"][0]),
    }
    nc = bacc.Bacc("TRN2", target_bir_lowering=False, num_devices=1)
    args = [nc.dram_tensor(n, v.shape, mybir.dt.from_np(v.dtype), kind="ExternalInput").ap()
            for n, v in arrays.items()]
    outT = nc.dram_tensor("outT", (DK, P, SEQ), F32, kind="ExternalOutput").ap()
    gates = nc.dram_tensor("gates", (2 * DK, P, T), F32, kind="Internal").ap()
    build(nc, *args, gates, outT)
    got = run_bass_kernel_spmd(nc, [arrays], core_ids=[0]).results[0]["outT"].reshape(D, SEQ)
    result = np.empty((SEQ, D), np.float32)
    result[real] = got.T
    return result[None]
```
